# Optimizing a Trainium2 kernel written in Bass

```python
import jax, jax.numpy as jnp
from jax import lax
import numpy as np
import math

D_MODEL = 1024
BATCH = 1
SEQ = 512
DEPTH = 1

MIX_WIDTH = D_MODEL
POOL_WIDTH = D_MODEL // 4
POOL_WINDOWS = (2, 4, 8, 16)
POOL_GROUP = POOL_WIDTH // len(POOL_WINDOWS)
HEAD_DIM = 64
ATTN_WIDTH = MIX_WIDTH - POOL_WIDTH
N_HEADS = ATTN_WIDTH // HEAD_DIM
DILATED_CONFIGS = ((128, 1), (512, 4), (2048, 16))
BLOCK = 128
ROPE_THETA = 10000.0
IN_WIDTH = POOL_WIDTH + 3 * ATTN_WIDTH
_FF_RAW = -(-8 * D_MODEL // 3)
D_FF = ((_FF_RAW + 255) // 256) * 256
EPS = 1e-6


def rms_norm(x, g):
    xf = x.astype(jnp.float32)
    y = xf * lax.rsqrt(jnp.mean(xf * xf, axis=-1, keepdims=True) + EPS)
    return (y * g.astype(jnp.float32)).astype(x.dtype)

def rope(x, pos):
    half = x.shape[-1] // 2
    freqs = ROPE_THETA ** (-jnp.arange(half, dtype=jnp.float32) * (2.0 / x.shape[-1]))
    ang = pos.astype(jnp.float32)[:, None] * freqs[None, :]
    cos = jnp.cos(ang)[None, :, None, :]
    sin = jnp.sin(ang)[None, :, None, :]
    xf = x.astype(jnp.float32)
    x1, x2 = xf[..., :half], xf[..., half:]
    out = jnp.concatenate([x1 * cos - x2 * sin, x2 * cos + x1 * sin], axis=-1)
    return out.astype(x.dtype)

def multi_scale_pool(u, w_pool, pool_scale):
    B, S, _ = u.shape
    ug = u.astype(jnp.float32).reshape(B, S, len(POOL_WINDOWS), POOL_GROUP)
    csum = lax.cumsum(ug, axis=1)
    t = jnp.arange(S)
    outs = []
    for gi, win in enumerate(POOL_WINDOWS):
        cg = csum[:, :, gi]
        shifted = jnp.pad(cg, ((0, 0), (win, 0), (0, 0)))[:, :S]
        cnt = jnp.minimum(t + 1, win).astype(jnp.float32)[None, :, None]
        outs.append((cg - shifted) / cnt - ug[:, :, gi])
    d = jnp.stack(outs, axis=2)
    y = jnp.einsum('bsgc,gcd->bsgd', d, w_pool.astype(jnp.float32))
    y = y.reshape(B, S, POOL_WIDTH) * pool_scale.astype(jnp.float32)
    return y.astype(u.dtype)

def dilated_branch(q, k, v, window, dilation):
    B, S, H, Dh = q.shape
    L = S // dilation
    nb = -(-L // BLOCK)
    Lp = nb * BLOCK
    w_sub = window // dilation

    def to_sub(a):
        a = a.reshape(B, L, dilation, H, Dh).transpose(0, 2, 1, 3, 4)
        return jnp.pad(a, ((0, 0), (0, 0), (0, Lp - L), (0, 0), (0, 0)))

    qs = to_sub(q).reshape(B, dilation, nb, BLOCK, H, Dh)
    kp = jnp.pad(to_sub(k), ((0, 0), (0, 0), (BLOCK, 0), (0, 0), (0, 0)))
    vp = jnp.pad(to_sub(v), ((0, 0), (0, 0), (BLOCK, 0), (0, 0), (0, 0)))

    def band(a):
        prev = a[:, :, :Lp].reshape(B, dilation, nb, BLOCK, H, Dh)
        cur = a[:, :, BLOCK:].reshape(B, dilation, nb, BLOCK, H, Dh)
        return jnp.concatenate([prev, cur], axis=3)

    kb, vb = band(kp), band(vp)
    scale = 1.0 / np.sqrt(Dh).astype(np.float32)
    s = jnp.einsum('brnqhd,brnkhd->brnhqk', qs.astype(jnp.float32), kb.astype(jnp.float32)) * scale

    qi = jnp.arange(BLOCK)[:, None]
    kj = jnp.arange(2 * BLOCK)[None, :]
    dist = qi + BLOCK - kj
    blk = jnp.arange(nb)[:, None, None]
    valid = (dist >= 0) & (dist <= w_sub) & (blk * BLOCK + kj - BLOCK >= 0)
    s = jnp.where(valid[None, None, :, None], s, -jnp.inf)

    m = jnp.max(s, axis=-1, keepdims=True)
    e = jnp.exp(s - m)
    den = jnp.sum(e, axis=-1, keepdims=True)
    lse = (m + jnp.log(den))[..., 0]
    o = jnp.einsum('brnhqk,brnkhd->brnqhd', e / den, vb.astype(jnp.float32))

    o = o.reshape(B, dilation, Lp, H, Dh)[:, :, :L].transpose(0, 2, 1, 3, 4).reshape(B, S, H, Dh)
    lse = lse.transpose(0, 1, 2, 4, 3).reshape(B, dilation, Lp, H)[:, :, :L]
    lse = lse.transpose(0, 2, 1, 3).reshape(B, S, H)
    return o, lse

def dilated_attention(q, k, v):
    outs, lses = [], []
    for window, dilation in DILATED_CONFIGS:
        o, lse = dilated_branch(q, k, v, window, dilation)
        outs.append(o)
        lses.append(lse)
    w = jax.nn.softmax(jnp.stack(lses, axis=0), axis=0)
    o = jnp.sum(w[..., None] * jnp.stack(outs, axis=0), axis=0)
    return o.astype(q.dtype)

def first_inputs(seed: int = 0) -> dict:
    key = jax.random.key(seed)
    ks = jax.random.split(key, 13)
    f32 = jnp.float32
    nrm = lambda k, shape, s: jax.random.normal(k, shape, f32) * s
    return {
        "x": jax.random.normal(ks[0], (BATCH, SEQ, D_MODEL), f32),
        "ln_pre_mix": 1.0 + nrm(ks[1], (DEPTH, D_MODEL), 0.05),
        "w_in": nrm(ks[2], (DEPTH, D_MODEL, IN_WIDTH), D_MODEL ** -0.5),
        "w_pool": nrm(ks[3], (DEPTH, len(POOL_WINDOWS), POOL_GROUP, POOL_GROUP), POOL_GROUP ** -0.5),
        "pool_scale": 1.0 + nrm(ks[4], (DEPTH, POOL_WIDTH), 0.1),
        "w_out": nrm(ks[5], (DEPTH, MIX_WIDTH, D_MODEL), MIX_WIDTH ** -0.5),
        "ln_post_mix": 1.0 + nrm(ks[6], (DEPTH, D_MODEL), 0.05),
        "ln_pre_ffn": 1.0 + nrm(ks[7], (DEPTH, D_MODEL), 0.05),
        "w_gate": nrm(ks[8], (DEPTH, D_MODEL, D_FF), D_MODEL ** -0.5),
        "w_up": nrm(ks[9], (DEPTH, D_MODEL, D_FF), D_MODEL ** -0.5),
        "w_down": nrm(ks[10], (DEPTH, D_FF, D_MODEL), D_FF ** -0.5),
        "ln_post_ffn": 1.0 + nrm(ks[11], (DEPTH, D_MODEL), 0.05),
    }

def first_block(x, ln_pre_mix, w_in, w_pool, pool_scale, w_out, ln_post_mix,
              ln_pre_ffn, w_gate, w_up, w_down, ln_post_ffn):
    B, S, _ = x.shape
    pos = jnp.arange(S)
    for l in range(DEPTH):
        h = rms_norm(x, ln_pre_mix[l])
        proj = h @ w_in[l]
        u_pool = proj[..., :POOL_WIDTH]
        q = proj[..., POOL_WIDTH:POOL_WIDTH + ATTN_WIDTH].reshape(B, S, N_HEADS, HEAD_DIM)
        k = proj[..., POOL_WIDTH + ATTN_WIDTH:POOL_WIDTH + 2 * ATTN_WIDTH].reshape(B, S, N_HEADS, HEAD_DIM)
        v = proj[..., POOL_WIDTH + 2 * ATTN_WIDTH:].reshape(B, S, N_HEADS, HEAD_DIM)
        q, k = rope(q, pos), rope(k, pos)
        pool_out = multi_scale_pool(u_pool, w_pool[l], pool_scale[l])
        attn_out = dilated_attention(q, k, v).reshape(B, S, ATTN_WIDTH)
        mix = jnp.concatenate([pool_out, attn_out], axis=-1) @ w_out[l]
        x = x + rms_norm(mix, ln_post_mix[l])
        h = rms_norm(x, ln_pre_ffn[l])
        f = (jax.nn.silu(h @ w_gate[l]) * (h @ w_up[l])) @ w_down[l]
        x = x + rms_norm(f, ln_post_ffn[l])
    return x


CHUNK = 64
Q_BLOCK = 128
H_DIFF = 4
H_FOX = 6
H_CHUNK = 6
N_PREV_CHUNKS = 8
REL_CLIP = 128
D_FF_2 = 2816
CONV_WIDTH = 3
PLE_DIM = 256
NEG_INF = -1e30

W_DIFF = H_DIFF * HEAD_DIM
W_FOX = H_FOX * HEAD_DIM
W_CHUNK = H_CHUNK * HEAD_DIM
MIX_WIDTH_2 = W_DIFF + W_FOX + W_CHUNK
IN_SIZES = (W_DIFF,) * 5 + (W_FOX,) * 3 + (H_FOX,) + (W_CHUNK,) * 3
IN_COLS = sum(IN_SIZES)
IN_SPLITS = tuple(int(c) for c in np.cumsum(IN_SIZES)[:-1])
ALIBI_SLOPES = tuple(2.0 ** (-8.0 * (h + 1) / H_DIFF) for h in range(H_DIFF))


def rms_norm_2(x, g):
    xf = x.astype(jnp.float32)
    y = xf * lax.rsqrt(jnp.mean(xf * xf, axis=-1, keepdims=True) + EPS)
    return (y * g.astype(jnp.float32)).astype(x.dtype)

def split_heads(t, n_heads):
    return t.reshape(t.shape[0], t.shape[1], n_heads, HEAD_DIM)

def query_blocks(q):
    b, s = q.shape[0], q.shape[1]
    q = q.reshape((b, s // Q_BLOCK, Q_BLOCK) + q.shape[2:])
    return jnp.swapaxes(q, 0, 1)

def merge_blocks(o):
    nb, b, qb, h, d = o.shape
    return jnp.swapaxes(o, 0, 1).reshape(b, nb * qb, h * d)

def diff_attention(q1, q2, k1, k2, v, lam, subln_g, lam_init):
    S = k1.shape[1]
    slopes = jnp.asarray(ALIBI_SLOPES, jnp.float32)
    kpos = jnp.arange(S)
    scale = HEAD_DIM ** -0.5

    def block(args):
        q1b, q2b, blk = args
        qpos = blk * Q_BLOCK + jnp.arange(Q_BLOCK)
        dist = jnp.abs(qpos[:, None] - kpos[None, :]).astype(jnp.float32)
        bias = -slopes[:, None, None] * dist
        allowed = (kpos[None, :] // CHUNK) <= (qpos[:, None] // CHUNK)

        def probs(qb, k):
            s = jnp.einsum('bqhd,bkhd->bhqk', qb, k).astype(jnp.float32) * scale + bias
            s = jnp.where(allowed, s, NEG_INF)
            return jax.nn.softmax(s, axis=-1)

        a = probs(q1b, k1) - lam * probs(q2b, k2)
        return jnp.einsum('bhqk,bkhd->bqhd', a.astype(v.dtype), v)

    nb = S // Q_BLOCK
    o = lax.map(block, (query_blocks(q1), query_blocks(q2), jnp.arange(nb)))
    o = rms_norm_2(o, subln_g) * (1.0 - lam_init)
    return merge_blocks(o)

def forgetting_attention(q, k, v, log_f):
    B, S, H, _ = q.shape
    F = jnp.cumsum(log_f, axis=1)
    F_k = jnp.transpose(F, (0, 2, 1))
    F_q = jnp.transpose(query_blocks(F), (0, 1, 3, 2))
    kpos = jnp.arange(S)
    scale = HEAD_DIM ** -0.5

    def block(args):
        qb, fq, blk = args
        qpos = blk * Q_BLOCK + jnp.arange(Q_BLOCK)
        s = jnp.einsum('bqhd,bkhd->bhqk', qb, k).astype(jnp.float32) * scale
        s = s + fq[..., None] - F_k[:, :, None, :]
        allowed = kpos[None, :] <= qpos[:, None]
        s = jnp.where(allowed, s, NEG_INF)
        pr = jax.nn.softmax(s, axis=-1)
        return jnp.einsum('bhqk,bkhd->bqhd', pr.astype(v.dtype), v)

    nb = S // Q_BLOCK
    o = lax.map(block, (query_blocks(q), F_q, jnp.arange(nb)))
    return merge_blocks(o)

def chunk_band(t):
    b, s, h, d = t.shape
    nc = s // CHUNK
    tc = t.reshape(b, nc, CHUNK, h, d)
    tp = jnp.pad(tc, ((0, 0), (N_PREV_CHUNKS, 0), (0, 0), (0, 0), (0, 0)))
    return jnp.concatenate([tp[:, j:j + nc] for j in range(N_PREV_CHUNKS + 1)], axis=2)

def chunk_attention(q, k, v, rel_table):
    B, S, H, d = q.shape
    nc = S // CHUNK
    band_len = (N_PREV_CHUNKS + 1) * CHUNK
    qc = q.reshape(B, nc, CHUNK, H, d)
    kb = chunk_band(k)
    vb = chunk_band(v)
    qq = np.arange(CHUNK)[:, None]
    kk = np.arange(band_len)[None, :]
    rel = N_PREV_CHUNKS * CHUNK + qq - kk
    idx = np.clip(rel, -REL_CLIP, REL_CLIP) + REL_CLIP
    bias = rel_table[:, idx].astype(jnp.float32)
    key_chunk = (jnp.arange(nc)[:, None] - N_PREV_CHUNKS
                 + (jnp.arange(band_len) // CHUNK)[None, :])
    valid = (key_chunk >= 0)[:, None, None, :]
    s = jnp.einsum('bcqhd,bckhd->bchqk', qc, kb).astype(jnp.float32) * (HEAD_DIM ** -0.5) + bias
    s = jnp.where(valid, s, NEG_INF)
    pr = jax.nn.softmax(s, axis=-1)
    o = jnp.einsum('bchqk,bckhd->bcqhd', pr.astype(v.dtype), vb)
    return o.reshape(B, S, H * d)

def conv_gated_mlp(h, w_up, conv_w, conv_b, w_down):
    u = h @ w_up
    S = u.shape[1]
    up = jnp.pad(u, ((0, 0), (CONV_WIDTH - 1, 0), (0, 0)))
    c = conv_b
    for j in range(CONV_WIDTH):
        c = c + conv_w[j] * up[:, j:j + S]
    gate, val = jnp.split(c, 2, axis=-1)
    return (jax.nn.silu(gate) * val) @ w_down

def second_inputs(seed: int = 0) -> dict:
    key = jax.random.key(seed)
    ks = jax.random.split(key, 20)
    f32 = jnp.float32
    nrm = lambda k, shape, s: jax.random.normal(k, shape, f32) * s
    gain = lambda k, shape: 1.0 + 0.05 * jax.random.normal(k, shape, f32)
    return {
        "x": jax.random.normal(ks[0], (BATCH, SEQ, D_MODEL), f32),
        "p": jax.random.normal(ks[1], (DEPTH, BATCH, SEQ, PLE_DIM), f32),
        "ln_mix": gain(ks[2], (DEPTH, D_MODEL)),
        "w_in": nrm(ks[3], (DEPTH, D_MODEL, IN_COLS), D_MODEL ** -0.5),
        "qk_gain": gain(ks[4], (DEPTH, 6, HEAD_DIM)),
        "lam_params": nrm(ks[5], (DEPTH, 4, HEAD_DIM), 0.1),
        "subln_gain": gain(ks[6], (DEPTH, HEAD_DIM)),
        "fgate_bias": jax.random.uniform(ks[7], (DEPTH, H_FOX), f32, 1.0, 4.0),
        "rel_bias": nrm(ks[8], (DEPTH, H_CHUNK, 2 * REL_CLIP + 1), 0.1),
        "w_out": nrm(ks[9], (DEPTH, MIX_WIDTH_2, D_MODEL), MIX_WIDTH_2 ** -0.5),
        "ln_ffn": gain(ks[10], (DEPTH, D_MODEL)),
        "w_up": nrm(ks[11], (DEPTH, D_MODEL, 2 * D_FF_2), D_MODEL ** -0.5),
        "conv_w": nrm(ks[12], (DEPTH, CONV_WIDTH, 2 * D_FF_2), CONV_WIDTH ** -0.5),
        "conv_b": nrm(ks[13], (DEPTH, 2 * D_FF_2), 0.02),
        "w_down": nrm(ks[14], (DEPTH, D_FF_2, D_MODEL), D_FF_2 ** -0.5),
        "ln_ple": gain(ks[15], (DEPTH, D_MODEL)),
        "w_ple_gate": nrm(ks[16], (DEPTH, D_MODEL, D_MODEL), D_MODEL ** -0.5),
        "w_ple_proj": nrm(ks[17], (DEPTH, PLE_DIM, D_MODEL), PLE_DIM ** -0.5),
    }

def second_block(x, p, ln_mix, w_in, qk_gain, lam_params, subln_gain, fgate_bias, rel_bias,
              w_out, ln_ffn, w_up, conv_w, conv_b, w_down, ln_ple, w_ple_gate, w_ple_proj):
    h = x
    for i in range(DEPTH):
        hn = rms_norm_2(h, ln_mix[i])
        z = hn @ w_in[i]
        (q1, q2, k1, k2, va, qf, kf, vf, fg, qc, kc, vc) = jnp.split(z, IN_SPLITS, axis=-1)
        g = qk_gain[i]
        q1 = rms_norm_2(split_heads(q1, H_DIFF), g[0])
        q2 = rms_norm_2(split_heads(q2, H_DIFF), g[0])
        k1 = rms_norm_2(split_heads(k1, H_DIFF), g[1])
        k2 = rms_norm_2(split_heads(k2, H_DIFF), g[1])
        va = split_heads(va, H_DIFF)
        lp = lam_params[i].astype(jnp.float32)
        lam_init = 0.8 - 0.6 * math.exp(-0.3 * i)
        lam = jnp.exp(jnp.sum(lp[0] * lp[1])) - jnp.exp(jnp.sum(lp[2] * lp[3])) + lam_init
        o_a = diff_attention(q1, q2, k1, k2, va, lam, subln_gain[i], lam_init)
        qf = rms_norm_2(split_heads(qf, H_FOX), g[2])
        kf = rms_norm_2(split_heads(kf, H_FOX), g[3])
        vf = split_heads(vf, H_FOX)
        log_f = jax.nn.log_sigmoid(fg.astype(jnp.float32) + fgate_bias[i].astype(jnp.float32))
        o_b = forgetting_attention(qf, kf, vf, log_f)
        qc = rms_norm_2(split_heads(qc, H_CHUNK), g[4])
        kc = rms_norm_2(split_heads(kc, H_CHUNK), g[5])
        vc = split_heads(vc, H_CHUNK)
        o_c = chunk_attention(qc, kc, vc, rel_bias[i])
        h = h + jnp.concatenate([o_a, o_b, o_c], axis=-1) @ w_out[i]
        h = h + conv_gated_mlp(rms_norm_2(h, ln_ffn[i]), w_up[i], conv_w[i], conv_b[i], w_down[i])
        gate = jax.nn.sigmoid(rms_norm_2(h, ln_ple[i]) @ w_ple_gate[i])
        h = h + (p[i] @ w_ple_proj[i]) * gate
    return h


def setup_inputs(seed=0):
    out = dict(first_inputs(seed))
    for name, value in second_inputs(seed + 1).items():
        if name != "x":
            out[name + "_2"] = value
    return out


def reference(
    x, ln_pre_mix, w_in, w_pool, pool_scale, w_out, ln_post_mix, ln_pre_ffn, w_gate, w_up,
    w_down, ln_post_ffn, p_2, ln_mix_2, w_in_2, qk_gain_2, lam_params_2, subln_gain_2,
    fgate_bias_2, rel_bias_2, w_out_2, ln_ffn_2, w_up_2, conv_w_2, conv_b_2, w_down_2, ln_ple_2,
    w_ple_gate_2, w_ple_proj_2,
):
    x = first_block(
        x, ln_pre_mix, w_in, w_pool, pool_scale, w_out, ln_post_mix, ln_pre_ffn, w_gate, w_up,
        w_down, ln_post_ffn,
    )
    return second_block(
        x, p_2, ln_mix_2, w_in_2, qk_gain_2, lam_params_2, subln_gain_2, fgate_bias_2,
        rel_bias_2, w_out_2, ln_ffn_2, w_up_2, conv_w_2, conv_b_2, w_down_2, ln_ple_2,
        w_ple_gate_2, w_ple_proj_2,
    )


_drawn_inputs = setup_inputs


def setup_inputs(seed=0):
    import zlib

    import numpy as np

    out = dict(_drawn_inputs(seed))
    spreads = {}
    factors = {'qk_gain_2': 3.888,
     'lam_params_2': 8.0,
     'subln_gain_2': 5.3,
     'rel_bias_2': 8.0,
     'conv_b_2': 6.306,
     'ln_ple_2': 38.568,
     'ln_ffn_2': 3.699}
    for name, (base, spread) in spreads.items():
        noise = np.random.default_rng([zlib.crc32(name.encode()), seed]).standard_normal(out[name].shape)
        drawn = base * np.exp(spread * noise) if base else spread * noise
        out[name] = __import__('jax').numpy.asarray(drawn.astype(out[name].dtype))
    for name, factor in factors.items():
        out[name] = (out[name] * factor).astype(out[name].dtype)
    return out
```

```python
from contextlib import ExitStack

import numpy as np

import concourse.bass as bass
from concourse import mybir

P = 128
S = 512
T = S // P
D = 1024
KB = D // P
FF = 2816
MT = FF // P
HD = 64
EPS = 1e-6
CW = 256
RB = 2
CHUNK = KB * CW
QUARTER = CHUNK // 4
KIB = 1024
BIG = 3.0e38
MASKED = -1.0e30

F32 = mybir.dt.float32
F32R = mybir.dt.float32r
ALU = mybir.AluOpType
ACT = mybir.ActivationFunctionType
AX = mybir.AxisListType.X

DIFF_Q1, DIFF_Q2, DIFF_K1, DIFF_K2, DIFF_V = (256 * i for i in range(5))
FOX = 1280
FOX_GATE = FOX + 3 * 384
CHK = FOX_GATE + 6
DIFF_SCALE = 1.0 - 0.2
LAM_INIT = 0.2

NORMED = ("diff_qk", "fox_qk", "chk_qk")
TURNED = ("q", "k") + NORMED


def interleave(main, filler):
    out, done = [], 0
    for n, step in enumerate(main):
        out.append(step)
        want = len(filler) * (n + 1) // len(main)
        out += filler[done:want]
        done = want
    return out + filler[done:]


def attention_steps(units, after):
    out = []
    for n in range(max([len(units) + 3] + [m + 4 for m in after])):
        if 0 <= n - 2 < len(units):
            out.append(("T", units[n - 2]))
        if n < len(units):
            out.append(("S", units[n]))
        if 0 <= n - 3 < len(units):
            out.append(("PV", units[n - 3]))
        out += after.get(n - 3, [])
    return out


def projection_steps(chunks, first, extra=None):
    projs = [(c, t) for c in range(first, len(chunks)) for t in range(T)]
    out = []
    for n in range(len(projs) + 2):
        if n < len(projs):
            out.append(("proj",) + projs[n])
        if 1 <= n <= len(projs):
            out.append(("rows",) + projs[n - 1])
        if n >= 2 and chunks[projs[n - 2][0]][0] in TURNED:
            out.append(("qkT",) + projs[n - 2])
        if n < len(projs) and chunks[projs[n][0]][0] in NORMED:
            out.append(("sum",) + projs[n])
        out += (extra or {}).get(n, [])
    return out


def block1_plan():
    chunks, steps = [], []

    def project(g):
        first = len(chunks)
        chunks.extend([("q", 256 + CW * g), ("k", 1024 + CW * g), ("v", 1792 + CW * g)])
        return projection_steps(chunks, first)

    steps += project(0)
    for g in range(3):
        units = [(4 * g + h, t) for h in range(4) for t in range(T)]
        after = {8 * j + 8: [("mixT", 2 + 2 * g + j)] for j in range(2)}
        if g < 2:
            filler = project(g + 1)
        else:
            c = len(chunks)
            chunks.append(("pool", 0))
            filler = [("poolproj", c, 0), ("poolproj", c, 1), ("poolmix", 0), ("poolmix", 1)]
        steps += interleave(attention_steps(units, after), filler)
    return chunks, steps


def block2_plan():
    chunks, steps = [], []

    six = [("q", h) for h in range(6)] + [("k", h) for h in range(6)]
    chunks += [("diff_v", DIFF_V, None)]
    chunks += [("diff_qk", col, tile) for col, tile in ((DIFF_Q1, 0), (DIFF_K1, 4), (DIFF_Q2, 2), (DIFF_K2, 6))]
    steps += projection_steps(chunks, 0)

    first = len(chunks)
    chunks += [("fox_vg", FOX + 1024, None), ("fox_v", FOX + 768, None)]
    chunks += [("fox_qk", FOX + CW * j, six[4 * j:4 * j + 4]) for j in range(3)]
    fox = projection_steps(chunks, first, {4: [("decay_abs",)], 5: [("decay_ln",)], 6: [("decay",)]})
    units = [(m, t) for m in range(8) for t in range(T)]
    after = {n: [] for n in range(40)}
    for h in range(4):
        after[8 * h + 7].append(("combine", h))
        after[8 * h + 8].append(("combine_scale", h))
        if h % 2:
            after[8 * h + 9].append(("mixT", h // 2))
    after = {n: a for n, a in after.items() if a}
    steps += interleave(attention_steps(units, after), fox)

    first = len(chunks)
    chunks += [("chk_v2", CHK + 896, None), ("chk_v", CHK + 768, None)]
    chunks += [("chk_qk", CHK + CW * j, six[4 * j:4 * j + 4]) for j in range(3)]
    chk = projection_steps(chunks, first)
    units = [(8 + m, t) for m in range(6) for t in range(T)]
    after = {8 * j + 8: [("mixT", 2 + j)] for j in range(3)}
    steps += interleave(attention_steps(units, after), chk)
    units = [(14 + m, t) for m in range(6) for t in range(T)]
    after = {8 * j + 8: [("mixT", 5 + j)] for j in range(3)}
    steps += attention_steps(units, after)
    return chunks, steps


class Counts:

    def __init__(self, steps, base):
        self.of, self.n = {}, dict(base)
        for s in steps:
            self.of[s] = dict(self.n)
            kind = s[0]
            if kind in ("proj", "poolproj", "poolmix"):
                self.n["product"] += 1
                self.n["bank"] += 1
            elif kind in ("qkT", "mixT", "decay"):
                self.n["turn"] += 1
            elif kind == "S":
                self.n["unit"] += 1


def two_blocks_kernel(nc, A, out):
    chunks1, steps1 = block1_plan()
    chunks2, steps2 = block2_plan()
    n1 = Counts(steps1, dict(product=0, bank=0, turn=0, unit=0))

    N_OUT, N_DOWN, N_UP = D // (RB * P), MT // RB, 2 * (MT // 2)
    C_OUT1 = len(chunks1)
    C_UP1 = C_OUT1 + N_OUT
    C_DOWN1 = C_UP1 + N_UP
    C_MIX2 = C_DOWN1 + N_DOWN
    C_OUT2 = C_MIX2 + len(chunks2)
    C_UP2 = C_OUT2 + N_OUT
    C_DOWN2 = C_UP2 + N_UP
    C_PP = C_DOWN2 + N_DOWN
    C_GATE = C_PP + 1
    C_END = C_GATE + D // CW

    G_OUT1 = n1.n["product"]
    G_UP1 = G_OUT1 + T * N_OUT
    G_DOWN1 = G_UP1 + 2 * N_UP
    G_MIX2 = G_DOWN1 + T * N_DOWN
    n2 = Counts(steps2, {**n1.n, "product": G_MIX2})
    G_OUT2 = n2.n["product"]
    G_UP2 = G_OUT2 + T * N_OUT
    G_DOWN2 = G_UP2 + 2 * N_UP
    G_PP = G_DOWN2 + T * N_DOWN
    G_GATE = G_PP + T

    class Mixer:
        pass

    mixers = []
    for b, (cnt, steps, chunks, c0, norm) in enumerate(((n1, steps1, chunks1, 0, 0), (n2, steps2, chunks2, C_MIX2, 2))):
        m = Mixer()
        m.b, m.cnt, m.steps, m.chunks, m.c0, m.norm = b, cnt, steps, chunks, c0, norm
        m.unit = {s[1]: cnt.of[s]["unit"] for s in steps if s[0] == "S"}
        m.consumed, m.rows, m.last_turn = {}, {}, {}
        for s in steps:
            if s[0] in ("proj", "poolproj"):
                m.consumed[s[1]] = cnt.of[s]["product"] + 1
                if chunks[s[1]][0] in TURNED:
                    m.rows[s[1], s[2]] = len(m.rows)
            if s[0] == "qkT":
                m.last_turn[s[1], s[2]] = cnt.of[s]["turn"] + 1
        m.turn_of_rows = [m.last_turn[k] for k in m.rows]
        mixers.append(m)

    with ExitStack() as ctx:
        def sb(name, shape, dt=F32):
            return ctx.enter_context(nc.sbuf_tensor(name, shape, dt))

        def sem(name):
            return ctx.enter_context(nc.semaphore(name))

        x = sb("x", [P, T, D])
        h_hi = sb("h_hi", [P, KB, S], F32R)
        h_lo = sb("h_lo", [P, KB, S], F32R)
        w_raw = sb("w_raw", [P, 2, CHUNK])
        w_hi = sb("w_hi", [P, 2, CHUNK], F32R)
        w_lo = sb("w_lo", [P, 2, CHUNK], F32R)
        gain_pre = sb("gain_pre", [P, D])
        ident = sb("ident", [P, P])
        tri = sb("tri", [P, P])
        ones = sb("ones", [P, P])
        causal = sb("causal", [P, S])
        conv_cols = sb("conv_cols", [P, 4, 2 * MT])
        scratch = sb("scratch", [P, 2, CW])
        squares = sb("squares", [P, CW])
        y_ss = sb("y_ss", [P, 2 * T])
        y_rs = sb("y_rs", [P, 2 * T])
        x_ss = sb("x_ss", [P, 5 * T])
        x_rs = sb("x_rs", [P, 5 * T])
        den = sb("den", [P, 8])
        neg_max = sb("neg_max", [P, 8])
        rden = sb("rden", [P, 8])
        qk_ss = sb("qk_ss", [P, 2, 4])
        qk_rs = sb("qk_rs", [P, 2, 4])
        half_neg = sb("half_neg", [P, 4])
        gcol = sb("gcol", [P, 8])
        fcol = sb("fcol", [HD + 2, 2])
        lam = sb("lam", [P, 8])
        den_c = sb("den_c", [P, T])
        gate_bias = sb("gate_bias", [P, 6])
        pool_inv = sb("pool_inv", [P, 2, 16])
        pool_gain = sb("pool_gain", [P, 2])
        decay = sb("decay", [P, 2, T, 6])
        augq = sb("augq", [P, T, 6, 2])
        augk = sb("augk", [P, T, 6, 2])
        arena_kib = 98.5
        sb("arena", [P, int(arena_kib * KIB) // 4])
        arena_start = nc.sbuf_base - int(arena_kib * KIB)
        ps = ctx.enter_context(nc.psum_tensor("ps", [P, 8, 512], F32))

        def at(name, kib, shape, dt=F32):
            assert kib * KIB + int(np.prod(shape[1:])) * 4 <= arena_kib * KIB, name
            return nc.alloc_sbuf_tensor_at(name, shape, dt, offset=arena_start + int(kib * KIB))

        hid = at("hid", 0, [P, MT, S])
        st_hi = at("st_hi", 44, [P, 2, RB, S], F32R)
        st_lo = at("st_lo", 52, [P, 2, RB, S], F32R)
        y_scaled = at("y_scaled", 60, [P, 2, D])
        h_tok = at("h_tok", 68, [P, 2, D])
        junk = at("junk", 76, [P, D])
        act_gate = at("act_gate", 80, [P, 2, S])
        act_val = at("act_val", 84, [P, 2, S])
        p_tok = at("p_tok", 88, [P, T, 256])
        pT = at("pT", 92, [P, RB, S])
        conv_rows = at("conv_rows", 96, [2 * MT, 4, P])
        pp = at("pp", 0, [P, T, D])
        sig = at("sig", 16, [P, 2, CW])
        gain_post = at("gain_post", 94.5, [P, D])
        mixT = at("mixT", 0, [P, KB, S])
        qk1 = at("qk1", 16, [P, 2, 4, S])
        v1 = at("v1", 32, [P, 2, T, CW])
        prob1 = at("prob1", 40, [P, 3, S])
        probT1 = at("probT1", 46, [P, 2, S])
        work1 = at("work1", 50, [P, 2, 4 * (HD + 2)])
        otok1 = at("otok1", 55, [P, 2, T, P])
        pool_d = at("pool_d", 60, [P, 2, S])
        pool_u = at("pool_u", 64, [P, 2, S])
        pool_a = at("pool_a", 68, [P, S])
        pool_b = at("pool_b", 70, [P, S])
        log_count = at("log_count", 80, [P, S])
        rope_cos = at("rope_cos", 82, [P, T, HD])
        rope_sin = at("rope_sin", 83, [P, T, HD])
        pool_w = at("pool_w", 84, [P, 2, P])
        lam_in = at("lam_in", 85, [P, 2, 2, HD])
        lam_prod = at("lam_prod", 86, [P, 2, HD])
        qa = at("qa", 16, [P, 8, S])
        va = at("va", 32, [P, T, 384])
        prob2 = at("prob2", 38, [P, 3, S])
        probT2 = at("probT2", 44, [P, 2, S])
        work2 = at("work2", 48, [P, 2, 4 * (HD + 2)])
        otok2 = at("otok2", 50.5, [P, 2, T, P])
        od = at("od", 54.5, [P, T, P])
        table = at("table", 56.5, [P, 6, S])
        fx = at("fx", 68.5, [HD + 2, 12, S])
        vx = at("vx", 92.5, [P, T, 384])

        x_in = [sem(f"x_in{t}") for t in range(T)]
        gain_in = [sem(f"gain_in{n}") for n in range(7)]
        const_in = sem("const_in")
        heads_in = sem("heads_in")
        table_in = sem("table_in")
        bias_in = sem("bias_in")
        conv_in = sem("conv_in")
        p_in = sem("p_in")
        out_in_dram = sem("out_in_dram")
        raw_in = [sem("raw_in0"), sem("raw_in1")]
        hi_done = sem("hi_done")
        lo_done = sem("lo_done")
        products_done = sem("products_done")
        constants_set = sem("constants_set")
        y_squared = sem("y_squared")
        y_rstd = sem("y_rstd")
        y_scaled_done = sem("y_scaled_done")
        x_added = sem("x_added")
        x_squared = sem("x_squared")
        x_rstd = sem("x_rstd")
        h_tok_done = sem("h_tok_done")
        h_turned = sem("h_turned")
        h_hi_done = sem("h_hi_done")
        h_lo_done = sem("h_lo_done")
        pool_chain = sem("pool_chain")
        dve_chain = sem("dve_chain")
        bank_read = sem("bank_read")
        sq_done = sem("sq_done")
        ss_done = sem("ss_done")
        rs_done = sem("rs_done")
        turned = sem("turned")
        slot_read = sem("slot_read")
        scores_done = sem("scores_done")
        biased = sem("biased")
        exp_done = sem("exp_done")
        prob_turned = sem("prob_turned")
        probT_done = sem("probT_done")
        pv_done = sem("pv_done")
        o_done = sem("o_done")
        combine_ss = sem("combine_ss")
        combine_rs = sem("combine_rs")
        combined = sem("combined")
        decay_in = sem("decay_in")
        decay_exp = sem("decay_exp")
        decay_sum = sem("decay_sum")
        decay_ln = sem("decay_ln")
        decay_log = sem("decay_log")
        lam_sum = sem("lam_sum")
        lam_exp = sem("lam_exp")
        pool_out = sem("pool_out")
        bias_masked = sem("bias_masked")
        st_hi_done = sem("st_hi_done")
        st_lo_done = sem("st_lo_done")
        gate_silu = sem("gate_silu")
        gate_tap = sem("gate_tap")
        gate_conv = sem("gate_conv")
        val_tap = sem("val_tap")
        hid_done = sem("hid_done")
        tap_chain = sem("tap_chain")
        small_turned = sem("small_turned")
        pT_done = sem("pT_done")
        conv_cols_done = sem("conv_cols_done")
        pp_done = sem("pp_done")
        sig_done = sem("sig_done")
        final_done = sem("final_done")
        N_CONST, N_HEADS = 12, 5

        def by_cols(slot):
            return [w[:, slot, :].rearrange("p (k n) -> p k n", k=KB) for w in (w_raw, w_hi, w_lo)]

        def by_rows(slot):
            return [w[:, slot, :].rearrange("p (k n) -> p k n", k=RB) for w in (w_raw, w_hi, w_lo)]

        def map_operands(b, m):
            low = HD * (m % 2)
            if b == 0:
                g, j, hh = m // 4 % 2, m % 4 // 2, m % 4
                return (qk1[low:low + HD, g, j, :], qk1[low:low + HD, g, 2 + j, :],
                        v1[:, g, :, HD * hh:HD * hh + HD], log_count)
            if m < 8:
                h, w = m // 2, m % 2
                low = HD * (h % 2)
                return (qa[low:low + HD, 2 * w + h // 2, :], qa[low:low + HD, 4 + 2 * w + h // 2, :],
                        va[:, :, HD * h:HD * h + HD], table[:, h, :])
            if m < 14:
                h = m - 8
                return fx[:, h, :], fx[:, 6 + h, :], vx[:, :, HD * h:HD * h + HD], causal
            h = m - 14
            return (qa[low:low + HD, h // 2, :], qa[low:low + HD, 3 + h // 2, :],
                    va[:, :, HD * h:HD * h + HD], table[:, h, :])

        def group_of(b, m):
            if b == 0:
                return [3 * (m // 4) + j for j in range(3)]
            kinds = ("diff_v", "diff_qk") if m < 8 else ("fox_vg", "fox_v", "fox_qk") if m < 14 else \
                ("chk_v2", "chk_v", "chk_qk")
            return [c for c, ch in enumerate(chunks2) if ch[0] in kinds]

        def rows_turned(mx, m):
            return max(mx.cnt.of[s]["turn"] + 1 for s in mx.steps if s[0] == "qkT" and s[1] in group_of(mx.b, m))

        def values_read(mx, m):
            return max(mx.cnt.of[s]["bank"] + 1 for s in mx.steps if s[0] == "proj" and s[1] in group_of(mx.b, m))

        def row_source(b, kb):
            if b == 0:
                pair = kb - 2
                return otok1[:, pair % 2, :, :], (2 * pair + 1, T - 1)
            if kb < 2:
                return od[:, :, :], None
            pair = kb + 2
            return otok2[:, pair % 2, :, :], (2 * pair + 1, T - 1)

        def turned_rows(t):
            return ps[:, 2 * t:2 * t + 2, :].rearrange("p a (k n) -> p (a k) n", n=P)

        def over_chunks(eng, n, chunk, start=0):
            pairs = max(0, (n - 1 - start) // 2)
            if pairs > 1:
                with eng.Fori(0, pairs) as i:
                    for s in range(2):
                        chunk(2 * i + (start + s), start + s, False)
            else:
                pairs = 0
            for j in range(start + 2 * pairs, n):
                chunk(j, j, j == n - 1)

        block = ctx.enter_context(nc.Block())

        @block.sync
        def _(sp):
            def load(c, slot, src, rows=False, first=False):
                if not first:
                    sp.wait_ge(lo_done, 4 * (c - 1))
                dst = (by_rows if rows else by_cols)(slot)[0]
                sp.dma_start(dst, src).then_inc(raw_in[slot], 16)

            def cols(w, col):
                return w.rearrange("(k p) n -> p k n", p=P)[:, :, bass.ds(col, CW)]

            def rows(w):
                return w.rearrange("(j k p) n -> j p k n", p=P, k=RB)

            def row_chunks(w, c0):
                n = w.shape[0] // (RB * P)
                odd = n % 2
                if odd:
                    load(c0, c0 % 2, rows(w)[0], rows=True)
                with sp.Fori(0, n // 2) as i:
                    for s in range(2):
                        load(2 * i + (c0 + odd + s), (c0 + odd + s) % 2, rows(w)[2 * i + (odd + s)], rows=True)

            def column_pairs(gate, up, off, c0):
                with sp.Fori(0, N_UP // 2) as i:
                    load(2 * i + c0, c0 % 2, cols(gate, CW * i))
                    load(2 * i + (c0 + 1), (c0 + 1) % 2, cols(up, CW * i + off))

            for t in range(T):
                sp.dma_start(x[:, t, :], A["x"][0, P * t:P * t + P, :]).then_inc(x_in[t], 16)
            for c, (kind, col) in enumerate(chunks1):
                load(c, c % 2, cols(A["w_in"][0], col), first=c < 2)
            row_chunks(A["w_out"][0], C_OUT1)
            column_pairs(A["w_gate"][0], A["w_up"][0], 0, C_UP1)
            row_chunks(A["w_down"][0], C_DOWN1)
            for j, (kind, col, _) in enumerate(chunks2):
                load(C_MIX2 + j, (C_MIX2 + j) % 2, cols(A["w_in_2"][0], col))
            row_chunks(A["w_out_2"][0], C_OUT2)
            column_pairs(A["w_up_2"][0], A["w_up_2"][0], FF, C_UP2)
            row_chunks(A["w_down_2"][0], C_DOWN2)
            load(C_PP, C_PP % 2, rows(A["w_ple_proj_2"][0])[0], rows=True)
            for j in range(D // CW):
                load(C_GATE + j, (C_GATE + j) % 2, cols(A["w_ple_gate_2"][0], CW * j))
            o = out[0].rearrange("(t p) n -> t p n", p=P)
            for j in range(D // CW):
                for t in range(T):
                    sp.wait_ge(final_done, T * j + t + 1)
                    sp.dma_start(o[t, :, CW * j:CW * j + CW], x[:, t, CW * j:CW * j + CW]).then_inc(out_in_dram, 16)
            sp.wait_ge(out_in_dram, 16 * T * (D // CW))

        @block.gpsimd
        def _(pool):
            chain = [0]

            def link(ins):
                chain[0] += 1
                ins.then_inc(pool_chain, 1)
                pool.wait_ge(pool_chain, chain[0])

            def rstd(out_, ss, n, width):
                link(pool.tensor_scalar(ss, ss, 1.0 / width, EPS, ALU.mult, ALU.add))
                return pool.tensor_tensor(out_, ss, half_neg[:, 0:n], ALU.pow)

            def gain(n, dst, name):
                a = A[name]
                pool.dma_start(dst, bass.AP(a.tensor, a.offset, [[0, P], [1, D]])).then_inc(gain_in[n], 16)

            gain(0, gain_pre[:, :], "ln_pre_mix")
            link(pool.memset(half_neg[:, :], -0.5))
            link(pool.memset(ident[:, :], 0.0))
            link(pool.affine_select(out=ident[:, :], in_=ident[:, :], compare_op=ALU.not_equal, fill=1.0,
                                    base=0, pattern=[[-1, P]], channel_multiplier=1))
            pool.memset(ones[:, :], 1.0)
            link(pool.memset(tri[:, :], 1.0))
            link(pool.affine_select(out=tri[:, :], in_=tri[:, :], compare_op=ALU.is_ge, fill=0.0,
                                    base=0, pattern=[[1, P]], channel_multiplier=-1))
            link(pool.memset(augq[:, :, :, 1], 1.0))
            link(pool.memset(augk[:, :, :, 0], 1.0))
            link(pool.memset(fcol[:, :], 1.0))
            pool.memset(pool_w[:, :, :], 0.0).then_inc(constants_set, 1)
            pool.wait_ge(constants_set, 1)
            for g in range(4):
                low = HD * (g % 2)
                pool.dma_start(pool_w[low:low + HD, g // 2, low:low + HD], A["w_pool"][0, g]).then_inc(heads_in, 16)
            pool.dma_start(fcol[0:HD, :], A["qk_gain_2"][0, 2:4].rearrange("n d -> d n"),
                           allow_slow_non_contiguous=True).then_inc(heads_in, 16)

            def norm(b, post):
                for s in range(T + 1):
                    if s < T and post:
                        n = T * (b - 1) + s
                        pool.wait_ge(y_squared, n + 1)
                        rstd(y_rs[:, n:n + 1], y_ss[:, n:n + 1], 1, D).then_inc(y_rstd, 1)
                    if s >= 1:
                        n = T * b + s - 1
                        pool.wait_ge(x_squared, n + 1)
                        rstd(x_rs[:, n:n + 1], x_ss[:, n:n + 1], 1, D).then_inc(x_rstd, 1)
                    if s < T and post:
                        n = T * (b - 1) + s
                        pool.wait_ge(y_scaled_done, n + 1)
                        pool.tensor_tensor(x[:, s, :], x[:, s, :], y_scaled[:, n % 2, :], ALU.add)\
                            .then_inc(x_added, 1)

            def mixer(mx):
                m_end = False
                for s in mx.steps:
                    kind = s[0]
                    if kind == "sum":
                        r = mx.rows[s[1], s[2]]
                        pool.wait_ge(ss_done, r + 1)
                        rstd(qk_rs[:, r % 2, :], qk_ss[:, r % 2, :], 4, HD).then_inc(rs_done, 1)
                    if kind == "proj" and mx.b == 1 and mx.chunks[s[1]][0] == "chk_v2" and s[2] == 0:
                        pool.wait_ge(biased, mx.unit[7, T - 1] + 1)
                        pool.dma_start(table[:, :, :], A["rel_table"]).then_inc(bias_in, 16)
                    if kind == "proj" and mx.b == 1 and mx.chunks[s[1]][0] == "chk_v" and s[2] == 0:
                        pool.wait_ge(bias_in, 16)
                        pool.memset(table[0:HD, :, S - HD:S], MASKED).then_inc(bias_masked, 1)
                    if kind == "combine":
                        pool.wait_ge(combine_ss, s[1] + 1)
                        rstd(lam[:, 4:8], den_c[:, :], 4, HD).then_inc(combine_rs, 1)
                    if kind == "poolproj":
                        window_means(s[2], mx.cnt.of[s]["bank"] + 1)

            def window_means(m, copied):
                u, d, a, b = pool_u[:, m, :], pool_d[:, m, :], pool_a, pool_b
                pool.wait_ge(bank_read, copied)

                def widen(dst, src, sh):
                    link(pool.tensor_copy(dst[:, 0:sh], src[:, 0:sh]))
                    link(pool.tensor_tensor(dst[:, sh:S], src[:, sh:S], src[:, 0:S - sh], ALU.add))

                widen(a[:, :], u, 1)
                widen(b[:, :], a[:, :], 2)
                if m:
                    widen(a[:, :], b[:, :], 4)
                    widen(b[:, :], a[:, :], 8)
                for half, src in ((0, a), (1, b)):
                    lo = HD * half
                    win = 2 << (2 * m + half)
                    link(pool.tensor_scalar(d[lo:lo + HD], src[lo:lo + HD, :], 1.0 / win, None, ALU.mult))
                    link(pool.tensor_tensor(d[lo:lo + HD, 0:16], src[lo:lo + HD, 0:16],
                                            pool_inv[lo:lo + HD, m, :], ALU.mult))
                pool.tensor_tensor(d, d, u, ALU.subtract).then_inc(pool_out, 1)

            pool.wait_ge(const_in, 16 * N_CONST)
            norm(0, False)
            mixer(mixers[0])
            gain(1, gain_post[:, :], "ln_post_mix")
            pool.wait_ge(h_tok_done, T)
            gain(2, gain_pre[:, :], "ln_pre_ffn")
            norm(1, True)
            pool.wait_ge(h_tok_done, 2 * T)
            gain(3, gain_post[:, :], "ln_post_ffn")
            gain(4, gain_pre[:, :], "ln_mix_2")
            norm(2, True)
            pool.wait_ge(h_lo_done, 3 * T)
            gain(5, gain_pre[:, :], "ln_ffn_2")
            pool.dma_start(table[:, 0:4, :], A["alibi"]).then_inc(table_in, 16)
            mixer(mixers[1])
            norm(3, False)
            pool.wait_ge(h_lo_done, 4 * T)
            pool.dma_start(conv_rows[:, 0:3, :], A["conv_w_2"][0].rearrange("j (m q) -> m j q", q=P))\
                .then_inc(conv_in, 16)
            pool.dma_start(conv_rows[:, 3, :], A["conv_b_2"][0].rearrange("(m q) -> m q", q=P)).then_inc(conv_in, 16)
            pool.dma_start(p_tok[:, :, :], A["p_2"][0, 0].rearrange("(t p) n -> p t n", p=P)).then_inc(p_in, 16)
            gain(6, gain_pre[:, :], "ln_ple_2")
            norm(4, False)

        @block.scalar
        def _(act):
            def const(dst, src, **kw):
                act.dma_start(dst, src, **kw).then_inc(const_in, 16)

            def bcast(a, n):
                return bass.AP(a.tensor, a.offset, [[0, P], [1, n]])

            const(rope_cos[:, :, :], A["rope_cos"])
            const(rope_sin[:, :, :], A["rope_sin"])
            const(log_count[:, :], A["log_count"])
            const(causal[:, :], A["causal"])
            const(lam_in[:, :, :, :], bcast(A["lam_params_2"], 4 * HD).rearrange("p (a b d) -> p a b d", a=2, b=2))
            for half in range(2):
                rows = slice(HD * half, HD * half + HD)
                const(gcol[rows, 0:6], A["qk_gain_2"][0].rearrange("n d -> d n"), allow_slow_non_contiguous=True)
                const(gcol[rows, 6:7], A["subln_gain_2"].rearrange("n d -> d n"), allow_slow_non_contiguous=True)
            const(gate_bias[:, :], bcast(A["fgate_bias_2"], 6))
            const(pool_inv[:, :, :], A["pool_inv"])
            const(pool_gain[:, :], A["pool_scale"][0].rearrange("(m p) -> p m", p=P), allow_slow_non_contiguous=True)

            def split_hi(c, slot, quarter, free):
                if quarter == 0:
                    act.wait_ge(raw_in[slot], 8 * c + (16 - 8 * slot))
                    if free is not None:
                        act.wait_ge(products_done, free)
                q = slice(QUARTER * quarter, QUARTER * quarter + QUARTER)
                act.activation(w_hi[:, slot, q], w_raw[:, slot, q], ACT.Copy).then_inc(hi_done, 1)

            def norm(b, post, added, g_y):
                def junk_free(ys, xs):
                    if ys > 0:
                        act.wait_ge(y_squared, ys)
                    if xs > 0:
                        act.wait_ge(x_squared, xs)

                ys0 = T * (b - 1) if post else T * min(b - 1, 2)
                for s in range(T + 2):
                    if s < T and post:
                        n = T * (b - 1) + s
                        act.wait_ge(products_done, g_y + s + 1)
                        junk_free(n, T * b + max(s - 1, 0))
                        act.activation(junk[:, :], ps[:, 2 * s:2 * s + 2, :].rearrange("p a n -> p (a n)"),
                                       ACT.Square, accum_out=y_ss[:, n:n + 1]).then_inc(y_squared, 1)
                    if 1 <= s <= T:
                        n = T * b + s - 1
                        if b == 0:
                            act.wait_ge(x_in[s - 1], 16)
                        else:
                            act.wait_ge(x_added, n - T + 1)
                        junk_free(ys0 + (min(s + 1, T) if post else 0), n)
                        act.activation(junk[:, :], x[:, s - 1, :], ACT.Square, accum_out=x_ss[:, n:n + 1])\
                            .then_inc(x_squared, 1)
                    if s >= 2:
                        t = s - 2
                        act.wait_ge(h_turned, T * b + t + 1)
                        act.activation(h_hi[:, :, P * t:P * t + P], turned_rows(t), ACT.Copy).then_inc(h_hi_done, 1)

            def mixer(mx):
                for s in mx.steps:
                    kind, of = s[0], mx.cnt.of[s]
                    if kind in ("proj", "poolproj"):
                        c = mx.c0 + s[1] + 1
                        free = mx.consumed[s[1] - 1] if s[1] else (G_MIX2 if mx.b else None)
                        for q in ([s[2]] if kind == "proj" else [2 * s[2], 2 * s[2] + 1]):
                            split_hi(c, c % 2, q, free)
                    if kind == "proj" and mx.b == 1 and (s[1], s[2]) in mx.rows:
                        r = mx.rows[s[1], s[2]]
                        act.wait_ge(products_done, of["product"] + 1)
                        if r >= 2:
                            act.wait_ge(ss_done, r - 1)
                        act.activation(scratch[:, r % 2, :], ps[:, of["bank"] % 2, 0:CW], ACT.Square)\
                            .then_inc(sq_done, 1)
                    if kind == "S":
                        u, kn = mx.unit[s[1]], P * (s[1][1] + 1)
                        prob = (prob1, prob2)[mx.b][:, u % 3, 0:kn]
                        act.wait_ge(biased, u + 1)
                        act.activation(prob, prob, ACT.Exp, bias=neg_max[:, u % 8:u % 8 + 1], scale=-1.0,
                                       accum_out=den[:, u % 8:u % 8 + 1]).then_inc(exp_done, 1)
                    if kind == "T":
                        u, kn = mx.unit[s[1]], P * (s[1][1] + 1)
                        act.wait_ge(prob_turned, u + 1)
                        if u >= 2:
                            act.wait_ge(pv_done, u - 1)
                        act.activation((probT1, probT2)[mx.b][:, u % 2, 0:kn], ps[:, 4 + u % 2, 0:kn], ACT.Copy)\
                            .then_inc(probT_done, 1)
                    if kind == "decay_abs":
                        act.wait_ge(decay_in, 1)
                        act.activation(decay[:, 1, :, :], decay[:, 1, :, :], ACT.Exp).then_inc(decay_exp, 1)
                    if kind == "decay_ln":
                        act.wait_ge(decay_sum, 1)
                        act.activation(decay[:, 1, :, :], decay[:, 1, :, :], ACT.Ln).then_inc(decay_ln, 1)

            def row_products(src, n, c0, g0, st0, ready=()):
                for s, v in ready:
                    act.wait_ge(s, v)

                def rows_hi(j, slot):
                    act.activation(st_hi[:, slot, :, :], src[:, bass.ds(2 * j, RB), :], ACT.Copy).then_inc(st_hi_done, 1)

                def chunk(j, jslot, last):
                    for t in range(T):
                        slot = (c0 + jslot + 1) % 2
                        split_hi(c0 + j + 1, slot, t, g0 + T * j)
                        if t == 0 and not last:
                            rows_hi(j + 1, (jslot + 1) % 2)

                rows_hi(0, 0)
                over_chunks(act, n, chunk)

            def swiglu(c0, g0):
                def pair(i, first):
                    for m in range(2):
                        for q in (2 * m, 2 * m + 1):
                            split_hi(2 * i + (c0 + 1), (c0 + 1) % 2, q, 4 * i + g0)
                        act.wait_ge(products_done, 4 * i + (g0 + m + 1))
                        if not first:
                            act.wait_ge(hid_done, 2 * i + (m - 1))
                        act.activation(act_gate[:, m, :], ps[:, m, :], ACT.Silu).then_inc(gate_silu, 1)
                    for q in range(4):
                        split_hi(2 * i + (c0 + 2), c0 % 2, q, 4 * i + (g0 + 2))

                pair(0, True)
                with act.Fori(1, N_UP // 2) as i:
                    pair(i, False)

            def conv_swiglu(c0, g0, hid0):
                act.wait_ge(conv_cols_done, 1)

                def tap(dst, m, src, col, sem_):
                    act.activation(dst[:, m, :], src, ACT.Identity, bias=conv_cols[:, 3, bass.ds(col, 1)],
                                   scale=conv_cols[:, 2, bass.ds(col, 1)]).then_inc(sem_, 1)

                def pair(i, first):
                    for m in range(2):
                        for q in (2 * m, 2 * m + 1):
                            split_hi(2 * i + (c0 + 1), (c0 + 1) % 2, q, 4 * i + g0)
                        act.wait_ge(products_done, 4 * i + (g0 + m + 1))
                        if not first:
                            act.wait_ge(hid_done, 2 * i + (hid0 + m - 1))
                        tap(act_gate, m, ps[:, m, :], 2 * i + m, gate_tap)
                    for q in range(4):
                        split_hi(2 * i + (c0 + 2), c0 % 2, q, 4 * i + (g0 + 2))
                    for m in range(2):
                        act.wait_ge(gate_conv, 2 * i + (m + 1))
                        act.activation(act_gate[:, m, :], act_gate[:, m, :], ACT.Silu).then_inc(gate_silu, 1)
                    for m in range(2):
                        act.wait_ge(products_done, 4 * i + (g0 + m + 3))
                        tap(act_val, m, ps[:, 2 + m, :], 2 * i + (MT + m), val_tap)

                pair(0, True)
                with act.Fori(1, N_UP // 2) as i:
                    pair(i, False)

            for q in range(4):
                split_hi(0, 0, q, None)
            act.wait_ge(lam_sum, 1)
            act.activation(lam[:, 2:4], lam[:, 0:2], ACT.Exp).then_inc(lam_exp, 1)
            norm(0, False, 0, 0)
            mixer(mixers[0])
            row_products(mixT, N_OUT, C_OUT1, G_OUT1, 0,
                         [(slot_read, n1.n["turn"]), (bank_read, n1.n["bank"]), (products_done, G_OUT1)])
            norm(1, True, 0, G_UP1 - T)
            swiglu(C_UP1, G_UP1)
            row_products(hid, N_DOWN, C_DOWN1, G_DOWN1, N_OUT, [(hid_done, MT), (products_done, G_DOWN1)])
            norm(2, True, 0, G_MIX2 - T)
            mixer(mixers[1])
            row_products(mixT, N_OUT, C_OUT2, G_OUT2, N_OUT + N_DOWN,
                         [(slot_read, n2.n["turn"]), (bank_read, n2.n["bank"]), (products_done, G_OUT2)])
            norm(3, False, 0, G_UP2 - T)
            act.wait_ge(small_turned, 1)
            act.activation(pT[:, :, :], ps[:, 4:6, :], ACT.Copy).then_inc(pT_done, 1)
            conv_swiglu(C_UP2, G_UP2, MT)
            row_products(hid, N_DOWN, C_DOWN2, G_DOWN2, 2 * N_OUT + N_DOWN, [(hid_done, 2 * MT), (products_done, G_DOWN2)])
            norm(4, False, 0, G_PP - T)
            act.activation(st_hi[:, 0, :, :], pT[:, :, :], ACT.Copy).then_inc(st_hi_done, 1)
            for t in range(T):
                split_hi(C_GATE, C_GATE % 2, t, G_PP)
            for t in range(T):
                act.wait_ge(products_done, G_PP + t + 1)
                act.activation(pp[:, t, :], ps[:, 2 * t:2 * t + 2, :].rearrange("p a n -> p (a n)"), ACT.Copy)\
                    .then_inc(pp_done, 1)
            for j in range(D // CW):
                for t in range(T):
                    n = T * j + t
                    if j + 1 < D // CW:
                        split_hi(C_GATE + j + 1, (C_GATE + j + 1) % 2, t, G_GATE + T * j)
                    act.wait_ge(products_done, G_GATE + n + 1)
                    if n >= 2:
                        act.wait_ge(final_done, n - 1)
                    act.activation(sig[:, n % 2, :], ps[:, n % 8, 0:CW], ACT.Sigmoid).then_inc(sig_done, 1)

        @block.vector
        def _(dve):
            chain = [0]

            def link(ins):
                chain[0] += 1
                ins.then_inc(dve_chain, 1)
                dve.wait_ge(dve_chain, chain[0])

            def split_lo(c, slot, quarter):
                dve.wait_ge(hi_done, 4 * c + (quarter + 1))
                q = slice(QUARTER * quarter, QUARTER * quarter + QUARTER)
                dve.tensor_tensor(w_lo[:, slot, q], w_raw[:, slot, q], w_hi[:, slot, q].bitcast(F32), ALU.subtract).then_inc(lo_done, 1)

            def norm(b, post, g_y):
                for s in range(T + 2):
                    if s < T and post:
                        n = T * (b - 1) + s
                        dve.wait_ge(y_rstd, n + 1)
                        if s == 0:
                            dve.wait_ge(gain_in[2 * b - 1], 16)
                        if n >= 2:
                            dve.wait_ge(x_added, n - 1)
                        dve.scalar_tensor_tensor(out=y_scaled[:, n % 2, :],
                                                 in0=ps[:, 2 * s:2 * s + 2, :].rearrange("p a n -> p (a n)"),
                                                 scalar=y_rs[:, n:n + 1], in1=gain_post[:, :],
                                                 op0=ALU.mult, op1=ALU.mult).then_inc(y_scaled_done, 1)
                    if s < T and b >= 3:
                        dve.wait_ge(products_done, g_y + s + 1)
                        dve.tensor_tensor(x[:, s, :], x[:, s, :],
                                          ps[:, 2 * s:2 * s + 2, :].rearrange("p a n -> p (a n)"), ALU.add)\
                            .then_inc(x_added, 1)
                    if 1 <= s <= T:
                        n = T * b + s - 1
                        dve.wait_ge(x_rstd, n + 1)
                        if s == 1:
                            dve.wait_ge(gain_in[(0, 2, 4, 5, 6)[b]], 16)
                        if n >= 2:
                            dve.wait_ge(h_turned, n - 1)
                        dve.scalar_tensor_tensor(out=h_tok[:, n % 2, :], in0=x[:, s - 1, :],
                                                 scalar=x_rs[:, n:n + 1], in1=gain_pre[:, :],
                                                 op0=ALU.mult, op1=ALU.mult).then_inc(h_tok_done, 1)
                    if s >= 2:
                        t = s - 2
                        dve.wait_ge(h_hi_done, T * b + t + 1)
                        dve.tensor_tensor(h_lo[:, :, P * t:P * t + P], turned_rows(t),
                                          h_hi[:, :, P * t:P * t + P].bitcast(F32), ALU.subtract)\
                            .then_inc(h_lo_done, 1)

            def heads4(ap):
                return ap.rearrange("p (h d) -> p h d", d=HD)

            def sum_squares(mx, s):
                r = mx.rows[s[1], s[2]]
                dve.wait_ge(sq_done, r + 1)
                if r >= 2:
                    dve.wait_ge(rs_done, r - 1)
                dve.tensor_reduce(qk_ss[:, r % 2, :], heads4(scratch[:, r % 2, :]), AX, ALU.add).then_inc(ss_done, 1)

            def rows_of_projection(mx, s):
                kind, of = mx.chunks[s[1]][0], mx.cnt.of["proj", s[1], s[2]]
                t, bank = s[2], ps[:, of["bank"] % 2, :]
                dve.wait_ge(products_done, of["product"] + 1)
                if (s[1], s[2]) in mx.rows:
                    r = mx.rows[s[1], s[2]]
                    if r >= 2:
                        dve.wait_ge(turned, mx.turn_of_rows[r - 2])
                if kind in ("q", "k"):
                    w = heads4(work1[:, r % 2, 0:CW])
                    sw = heads4(scratch[:, r % 2, :])
                    src = heads4(bank[:, 0:CW])
                    half = HD // 2
                    dve.tensor_tensor(w, src, rope_cos[:, t:t + 1, :].to_broadcast([P, 4, HD]), ALU.mult)
                    dve.tensor_tensor(sw[:, :, 0:half], src[:, :, half:HD],
                                      rope_sin[:, t:t + 1, 0:half].to_broadcast([P, 4, half]), ALU.mult)
                    link(dve.tensor_tensor(sw[:, :, half:HD], src[:, :, 0:half],
                                           rope_sin[:, t:t + 1, half:HD].to_broadcast([P, 4, half]), ALU.mult))
                    dve.tensor_tensor(w, w, sw, ALU.add).then_inc(bank_read, 1)
                elif kind == "v":
                    dve.tensor_copy(v1[:, s[1] // 3 % 2, t, :], bank[:, 0:CW]).then_inc(bank_read, 1)
                elif kind == "chk_v":
                    dve.tensor_copy(va[:, t, 0:P], bank[:, 0:P]).then_inc(bank_read, 1)
                elif kind == "diff_v":
                    dve.tensor_copy(va[:, t, 0:CW], bank[:, 0:CW]).then_inc(bank_read, 1)
                elif kind == "fox_v":
                    dve.tensor_copy(vx[:, t, 0:CW], bank[:, 0:CW]).then_inc(bank_read, 1)
                elif kind == "chk_v2":
                    dve.tensor_copy(va[:, t, P:384], bank[:, 0:CW]).then_inc(bank_read, 1)
                elif kind == "fox_vg":
                    dve.tensor_tensor(decay[:, 0, t, :], bank[:, P:P + 6], gate_bias[:, :], ALU.add)
                    dve.tensor_copy(vx[:, t, CW:384], bank[:, 0:P]).then_inc(bank_read, 1)
                else:
                    if kind == "fox_qk":
                        w = work2[:, r % 2, :].rearrange("p (h d) -> p h d", d=HD + 2)
                        for j in range(2):
                            which, h = mx.chunks[s[1]][2][2 * j]
                            aug = augq if which == "q" else augk
                            dve.tensor_copy(w[:, 2 * j:2 * j + 2, HD:HD + 2], aug[:, t, h:h + 2, :])
                        w = w[:, :, 0:HD]
                    else:
                        w = heads4(work2[:, r % 2, 0:CW])
                    dve.wait_ge(rs_done, r + 1)
                    dve.tensor_tensor(w, heads4(bank[:, 0:CW]),
                                      qk_rs[:, r % 2, :].rearrange("p (h o) -> p h o", o=1).to_broadcast([P, 4, HD]),
                                      ALU.mult).then_inc(bank_read, 1)

            def read_turned(mx, s, of):
                turn = ps[:, 7, :].rearrange("p (j n) -> p j n", n=P)
                dve.wait_ge(turned, of["turn"] + 1)
                if s[0] == "mixT":
                    if mx.b == 1 and s[1] < 2:
                        dve.tensor_scalar(mixT[:, s[1], :], ps[:, 7, :], gcol[:, 6:7], None, ALU.mult)\
                            .then_inc(slot_read, 1)
                    else:
                        dve.tensor_copy(mixT[:, s[1], :], ps[:, 7, :]).then_inc(slot_read, 1)
                    return
                chunk, tok = mx.chunks[s[1]], slice(P * s[2], P * s[2] + P)
                if chunk[0] in ("q", "k"):
                    first = 0 if chunk[0] == "q" else 2
                    dve.tensor_scalar(qk1[:, s[1] // 3 % 2, first:first + 2, tok], turn[:, 0:2, :],
                                      0.125 if first == 0 else 1.0, None, ALU.mult).then_inc(slot_read, 1)
                elif chunk[0] == "diff_qk":
                    g = 0 if chunk[2] < 4 else 1
                    dve.tensor_scalar(qa[:, chunk[2]:chunk[2] + 2, tok], turn[:, 0:2, :],
                                      gcol[:, g:g + 1], None, ALU.mult).then_inc(slot_read, 1)
                elif chunk[0] == "chk_qk":
                    for j in range(2):
                        which, h = chunk[2][2 * j]
                        tile, g = (h // 2, 4) if which == "q" else (3 + h // 2, 5)
                        ins = dve.tensor_scalar(qa[:, tile, tok], turn[:, j, :], gcol[:, g:g + 1], None, ALU.mult)
                    ins.then_inc(slot_read, 1)
                else:
                    for j in range(2):
                        which, h = chunk[2][2 * j]
                        tile, g = (h, 0) if which == "q" else (6 + h, 1)
                        ins = dve.tensor_scalar(fx[:, tile:tile + 2, tok], turn[0:HD + 2, 2 * j:2 * j + 2, :],
                                                fcol[:, g:g + 1], None, ALU.mult)
                    ins.then_inc(slot_read, 1)

            z_gate, e_gate = decay[:, 0, :, :], decay[:, 1, :, :]

            def decay_abs(mx):
                gates = max(mx.cnt.of[s]["bank"] for s in mx.steps if s[0] == "proj" and mx.chunks[s[1]][0] == "fox_vg")
                dve.wait_ge(bank_read, gates + 1)
                dve.scalar_tensor_tensor(out=e_gate, in0=z_gate, scalar=-1.0, in1=z_gate, op0=ALU.mult, op1=ALU.min)\
                    .then_inc(decay_in, 1)

            def decay_rows(of):
                dve.wait_ge(decay_ln, 1)
                dve.scalar_tensor_tensor(out=z_gate, in0=z_gate, scalar=0.0, in1=e_gate, op0=ALU.min, op1=ALU.subtract)\
                    .then_inc(decay_log, 1)
                dve.wait_ge(turned, of["turn"] + 1)
                f = ps[:, 7, 0:6 * T].rearrange("p (t h) -> p t h", t=T)
                dve.tensor_copy(augq[:, :, :, 0], f)
                dve.tensor_scalar(augk[:, :, :, 1], f, -1.0, None, ALU.mult).then_inc(slot_read, 1)
                dve.wait_ge(slot_read, of["turn"] + 1)

            def combine(mx, h):
                o = otok2[:, h % 2, :, :]
                low = HD * (h % 2)
                dst = od[:, :, low:low + HD]
                dve.wait_ge(o_done, mx.unit[2 * h + 1, T - 1] + 1)
                link(dve.scalar_tensor_tensor(out=dst, in0=o[:, :, HD:P], scalar=lam[:, 2:3], in1=o[:, :, 0:HD],
                                              op0=ALU.mult, op1=ALU.add))
                sq = squares[:, :].rearrange("p (t d) -> p t d", t=T)
                link(dve.tensor_tensor(sq, dst, dst, ALU.mult))
                dve.tensor_reduce(den_c[:, :], sq, AX, ALU.add).then_inc(combine_ss, 1)

            def combine_scale(h):
                low = HD * (h % 2)
                dst = od[:, :, low:low + HD]
                dve.wait_ge(combine_rs, h + 1)
                dve.tensor_tensor(dst, dst, lam[:, 4:8].rearrange("p (t o) -> p t o", o=1).to_broadcast([P, T, HD]),
                                  ALU.mult).then_inc(combined, 1)

            def mixer(mx):
                prob, otok = (prob1, prob2)[mx.b], (otok1, otok2)[mx.b]
                for s in mx.steps:
                    kind, of = s[0], mx.cnt.of[s]
                    if kind in ("proj", "poolproj"):
                        c = mx.c0 + s[1] + 1
                        for q in ([s[2]] if kind == "proj" else [2 * s[2], 2 * s[2] + 1]):
                            split_lo(c, c % 2, q)
                    if kind == "rows":
                        rows_of_projection(mx, s)
                    elif kind == "sum":
                        sum_squares(mx, s)
                    elif kind == "poolproj":
                        dve.wait_ge(products_done, of["product"] + 1)
                        dve.tensor_copy(pool_u[:, s[2], :], ps[:, of["bank"] % 2, :]).then_inc(bank_read, 1)
                    elif kind == "poolmix":
                        dve.wait_ge(products_done, of["product"] + 1)
                        dve.tensor_scalar(mixT[:, s[1], :], ps[:, of["bank"] % 2, :], pool_gain[:, s[1]:s[1] + 1],
                                          None, ALU.mult).then_inc(bank_read, 1)
                    elif kind in ("qkT", "mixT"):
                        read_turned(mx, s, of)
                    elif kind == "decay_abs":
                        decay_abs(mx)
                    elif kind == "decay_ln":
                        dve.wait_ge(decay_exp, 1)
                        dve.tensor_scalar(e_gate, e_gate, 1.0, None, ALU.add).then_inc(decay_sum, 1)
                    elif kind == "decay":
                        decay_rows(of)
                    elif kind == "combine":
                        combine(mx, s[1])
                    elif kind == "combine_scale":
                        combine_scale(s[1])
                    elif kind == "S":
                        (m, t), u = s[1], mx.unit[s[1]]
                        kn = P * (t + 1)
                        dve.wait_ge(scores_done, u + 1)
                        if mx.b == 1 and (m, t) == (0, 0):
                            dve.wait_ge(table_in, 16)
                        if mx.b == 1 and (m, t) == (14, 0):
                            dve.wait_ge(bias_masked, 1)
                        if u >= 3:
                            dve.wait_ge(prob_turned, u - 2)
                        dve.tensor_tensor_reduce(out=prob[:, u % 3, 0:kn], in0=ps[:, 2 + u % 2, 0:kn],
                                                 in1=map_operands(mx.b, m)[3][:, S - kn:S], scale=-1.0, scalar=BIG,
                                                 op0=ALU.add, op1=ALU.min, accum_out=neg_max[:, u % 8:u % 8 + 1])\
                            .then_inc(biased, 1)
                    elif kind == "T":
                        u = mx.unit[s[1]]
                        dve.wait_ge(exp_done, u + 1)
                        link_later(dve.reciprocal(rden[:, u % 8:u % 8 + 1], den[:, u % 8:u % 8 + 1]))
                    elif kind == "PV":
                        (m, t), u = s[1], mx.unit[s[1]]
                        dve.wait_ge(dve_chain, recips[u])
                        dve.wait_ge(pv_done, u + 1)
                        o = ps[:, 6, 0:HD]
                        dve.tensor_scalar(otok[:, m // 2 % 2, t, HD * (m % 2):HD * (m % 2) + HD], o,
                                          rden[:, u % 8:u % 8 + 1], None, ALU.mult).then_inc(o_done, 1)

            recips = []

            def link_later(ins):
                chain[0] += 1
                ins.then_inc(dve_chain, 1)
                recips.append(chain[0])

            def row_products(src, n, c0, g0, st0):
                def rows_lo(j, slot):
                    dve.wait_ge(st_hi_done, j + (st0 + 1))
                    dve.tensor_tensor(st_lo[:, slot, :, :], src[:, bass.ds(2 * j, RB), :],
                                      st_hi[:, slot, :, :].bitcast(F32), ALU.subtract).then_inc(st_lo_done, 1)

                def chunk(j, jslot, last):
                    for t in range(T):
                        split_lo(c0 + j + 1, (c0 + jslot + 1) % 2, t)
                        if t == 0 and not last:
                            rows_lo(j + 1, (jslot + 1) % 2)

                rows_lo(0, 0)
                over_chunks(dve, n, chunk)

            def swiglu(c0, g0):
                def pair(i):
                    for q in range(4):
                        split_lo(2 * i + (c0 + 1), (c0 + 1) % 2, q)
                    for q in range(4):
                        split_lo(2 * i + (c0 + 2), c0 % 2, q)
                    for m in range(2):
                        dve.wait_ge(gate_silu, 2 * i + (m + 1))
                        dve.wait_ge(products_done, 4 * i + (g0 + m + 3))
                        dve.tensor_tensor(hid[:, bass.ds(2 * i + m, 1), :].rearrange("p o n -> p (o n)"),
                                          act_gate[:, m, :], ps[:, 2 + m, :], ALU.mult).then_inc(hid_done, 1)

                with dve.Fori(0, N_UP // 2) as i:
                    pair(i)

            def conv_swiglu(c0, g0):
                def taps(dst, m, src, col, ready, count, chain0, done):
                    dve.wait_ge(ready, count)
                    dve.scalar_tensor_tensor(out=dst[:, m, 1:S], in0=src[:, 0:S - 1],
                                             scalar=conv_cols[:, 1, bass.ds(col, 1)], in1=dst[:, m, 1:S],
                                             op0=ALU.mult, op1=ALU.add).then_inc(tap_chain, 1)
                    dve.wait_ge(tap_chain, chain0)
                    return dve.scalar_tensor_tensor(out=dst[:, m, 2:S], in0=src[:, 0:S - 2],
                                                    scalar=conv_cols[:, 0, bass.ds(col, 1)], in1=dst[:, m, 2:S],
                                                    op0=ALU.mult, op1=ALU.add).then_inc(done, 1)

                with dve.Fori(0, N_UP // 2) as i:
                    for m in range(2):
                        for q in (2 * m, 2 * m + 1):
                            split_lo(2 * i + (c0 + 1), (c0 + 1) % 2, q)
                        taps(act_gate, m, ps[:, m, :], 2 * i + m, gate_tap, 2 * i + (m + 1), 6 * i + (m + 1), gate_conv)
                    for q in range(4):
                        split_lo(2 * i + (c0 + 2), c0 % 2, q)
                    for m in range(2):
                        taps(act_val, m, ps[:, 2 + m, :], 2 * i + (MT + m), val_tap, 2 * i + (m + 1),
                             6 * i + (2 * m + 3), tap_chain)
                        dve.wait_ge(tap_chain, 6 * i + (2 * m + 4))
                        dve.wait_ge(gate_silu, 2 * i + (MT + m + 1))
                        dve.tensor_tensor(hid[:, bass.ds(2 * i + m, 1), :].rearrange("p o n -> p (o n)"),
                                          act_gate[:, m, :], act_val[:, m, :], ALU.mult).then_inc(hid_done, 1)

            dve.wait_ge(const_in, 16 * N_CONST)
            dve.wait_ge(heads_in, 16 * N_HEADS)
            link(dve.tensor_tensor(lam_prod[:, :, :], lam_in[:, :, 0, :], lam_in[:, :, 1, :], ALU.mult))
            dve.tensor_reduce(lam[:, 0:2], lam_prod[:, :, :], AX, ALU.add).then_inc(lam_sum, 1)
            dve.tensor_scalar(gcol[:, 0:6:2], gcol[:, 0:6:2], 0.125, None, ALU.mult)
            dve.tensor_scalar(gcol[:, 6:7], gcol[:, 6:7], DIFF_SCALE, None, ALU.mult)
            dve.tensor_scalar(fcol[0:HD, 0:1], fcol[0:HD, 0:1], 0.125, None, ALU.mult)
            for q in range(4):
                split_lo(0, 0, q)
            dve.wait_ge(lam_exp, 1)
            link(dve.scalar_tensor_tensor(out=lam[:, 2:3], in0=lam[:, 3:4], scalar=-LAM_INIT, in1=lam[:, 2:3],
                                          op0=ALU.add, op1=ALU.subtract))
            norm(0, False, 0)
            mixer(mixers[0])
            dve.wait_ge(bank_read, n1.n["bank"])
            dve.wait_ge(slot_read, n1.n["turn"])
            row_products(mixT, N_OUT, C_OUT1, G_OUT1, 0)
            norm(1, True, G_UP1 - T)
            swiglu(C_UP1, G_UP1)
            dve.wait_ge(hid_done, MT)
            row_products(hid, N_DOWN, C_DOWN1, G_DOWN1, N_OUT)
            norm(2, True, G_MIX2 - T)
            mixer(mixers[1])
            dve.wait_ge(bank_read, n2.n["bank"])
            dve.wait_ge(slot_read, n2.n["turn"])
            row_products(mixT, N_OUT, C_OUT2, G_OUT2, N_OUT + N_DOWN)
            norm(3, False, G_UP2 - T)
            dve.wait_ge(small_turned, 2)
            dve.tensor_copy(conv_cols[:, :, :], ps[:, 6, 0:8 * MT].rearrange("p (j m) -> p j m", j=4))\
                .then_inc(conv_cols_done, 1)
            dve.wait_ge(conv_cols_done, 1)
            conv_swiglu(C_UP2, G_UP2)
            dve.wait_ge(hid_done, 2 * MT)
            row_products(hid, N_DOWN, C_DOWN2, G_DOWN2, 2 * N_OUT + N_DOWN)
            norm(4, False, G_PP - T)
            n_st = 2 * (N_OUT + N_DOWN)
            dve.wait_ge(st_hi_done, n_st + 1)
            dve.tensor_tensor(st_lo[:, 0, :, :], pT[:, :, :], st_hi[:, 0, :, :].bitcast(F32), ALU.subtract)\
                .then_inc(st_lo_done, 1)
            for t in range(T):
                split_lo(C_GATE, C_GATE % 2, t)
            for j in range(D // CW):
                for t in range(T):
                    n = T * j + t
                    if j + 1 < D // CW:
                        split_lo(C_GATE + j + 1, (C_GATE + j + 1) % 2, t)
                    dve.wait_ge(pp_done, t + 1)
                    dve.wait_ge(sig_done, n + 1)
                    link(dve.tensor_tensor(sig[:, n % 2, :], sig[:, n % 2, :], pp[:, t, CW * j:CW * j + CW], ALU.mult))
                    xs = x[:, t, CW * j:CW * j + CW]
                    dve.tensor_tensor(xs, xs, sig[:, n % 2, :], ALU.add).then_inc(final_done, 1)

        @block.tensor
        def _(pe):
            def products(out_, pairs):
                for n, (s_hi, s_lo, m_hi, m_lo) in enumerate(pairs):
                    pe.matmul(out_, s_hi, m_hi, start=(n == 0), stop=False)
                    pe.matmul(out_, s_hi, m_lo, start=False, stop=False)
                    mm = pe.matmul(out_, s_lo, m_hi, start=False, stop=(n == len(pairs) - 1))
                return mm

            def norm(b):
                for t in range(T):
                    n = T * b + t
                    pe.wait_ge(h_tok_done, n + 1)
                    for k in range(KB):
                        tr = pe.transpose(turned_rows(t)[:, k, :], h_tok[:, n % 2, P * k:P * k + P], ident[:, :])
                    tr.then_inc(h_turned, 1)

            def projection(bank, t, slot):
                _, hi, lo = by_cols(slot)
                tok = slice(P * t, P * t + P)
                return products(ps[:, bank, 0:CW],
                                [(h_hi[:, k, tok], h_lo[:, k, tok], hi[:, k, :], lo[:, k, :])
                                 for k in range(KB)])

            def turned_projection(bank, m, slot):
                _, hi, lo = by_cols(slot)
                col = slice(P * m, P * m + P)
                return products(ps[:, bank, :], [(hi[:, k, col], lo[:, k, col], h_hi[:, k, :], h_lo[:, k, :])
                                                 for k in range(KB)])

            def mixer(mx):
                prob, probT, work = (prob1, prob2)[mx.b], (probT1, probT2)[mx.b], (work1, work2)[mx.b]
                for s in mx.steps:
                    kind, of = s[0], mx.cnt.of[s]
                    if kind in ("proj", "poolproj", "poolmix"):
                        if kind != "poolmix":
                            c = mx.c0 + s[1]
                            if s[2] == 0:
                                pe.wait_ge(lo_done, 4 * (c + 1))
                            pe.wait_ge(h_lo_done, T * mx.norm + (s[2] + 1 if kind == "proj" else T))
                        if of["bank"] >= 2:
                            pe.wait_ge(bank_read, of["bank"] - 1)
                    if kind == "proj":
                        projection(of["bank"] % 2, s[2], c % 2).then_inc(products_done, 1)
                    elif kind == "poolproj":
                        turned_projection(of["bank"] % 2, s[2], c % 2).then_inc(products_done, 1)
                    elif kind == "poolmix":
                        pe.wait_ge(pool_out, s[1] + 1)
                        pe.wait_ge(heads_in, 16 * N_HEADS)
                        pe.matmul(ps[:, of["bank"] % 2, :], pool_w[:, s[1], :], pool_d[:, s[1], :],
                                  start=True, stop=True).then_inc(products_done, 1)
                    elif kind in ("qkT", "mixT", "decay"):
                        if of["turn"] >= 1:
                            pe.wait_ge(slot_read, of["turn"])
                        if kind == "qkT":
                            r = mx.rows[s[1], s[2]]
                            pe.wait_ge(bank_read, mx.cnt.of["proj", s[1], s[2]]["bank"] + 1)
                            if mx.chunks[s[1]][0] == "fox_qk":
                                for j in range(4):
                                    col = (HD + 2) * j
                                    tr = pe.transpose(ps[0:HD + 2, 7, P * j:P * j + P],
                                                      work[:, r % 2, col:col + HD + 2], ident[:, :])
                            else:
                                for j in range(2):
                                    tr = pe.transpose(ps[:, 7, P * j:P * j + P], work[:, r % 2, P * j:P * j + P],
                                                      ident[:, :])
                            tr.then_inc(turned, 1)
                        elif kind == "mixT":
                            src, last = row_source(mx.b, s[1])
                            if last is None:
                                pe.wait_ge(combined, 2 * s[1] + 2)
                            else:
                                pe.wait_ge(o_done, mx.unit[last] + 1)
                            for t in range(T):
                                tr = pe.transpose(ps[:, 7, P * t:P * t + P], src[:, t, :], ident[:, :])
                            tr.then_inc(turned, 1)
                        else:
                            pe.wait_ge(decay_log, 1)
                            for t in range(T):
                                for j in range(t + 1):
                                    mm = pe.matmul(ps[:, 7, 6 * t:6 * t + 6], (tri if j == t else ones)[:, :],
                                                   decay[:, 0, j, :], start=(j == 0), stop=(j == t))
                            mm.then_inc(turned, 1)
                    elif kind == "S":
                        (m, t), u = s[1], mx.unit[s[1]]
                        q, k, _, _ = map_operands(mx.b, m)
                        if t == 0:
                            pe.wait_ge(slot_read, rows_turned(mx, m))
                        if u >= 2:
                            pe.wait_ge(biased, u - 1)
                        pe.matmul(ps[:, 2 + u % 2, 0:P * (t + 1)], q[:, P * t:P * t + P], k[:, 0:P * (t + 1)],
                                  start=True, stop=True).then_inc(scores_done, 1)
                    elif kind == "T":
                        (m, t), u = s[1], mx.unit[s[1]]
                        pe.wait_ge(exp_done, u + 1)
                        if u >= 2:
                            pe.wait_ge(probT_done, u - 1)
                        for j in range(t + 1):
                            tr = pe.transpose(ps[:, 4 + u % 2, P * j:P * j + P], prob[:, u % 3, P * j:P * j + P],
                                              ident[:, :])
                        tr.then_inc(prob_turned, 1)
                    elif kind == "PV":
                        (m, t), u = s[1], mx.unit[s[1]]
                        v = map_operands(mx.b, m)[2]
                        if t == 0:
                            pe.wait_ge(bank_read, values_read(mx, m))
                        pe.wait_ge(probT_done, u + 1)
                        if u >= 1:
                            pe.wait_ge(o_done, u)
                        for j in range(t + 1):
                            mm = pe.matmul(ps[:, 6, 0:HD],
                                           probT[:, u % 2, P * j:P * j + P], v[:, j, :], start=(j == 0), stop=(j == t))
                        mm.then_inc(pv_done, 1)

            def row_products(n, c0, st0, banks_free):
                for s, v in banks_free:
                    pe.wait_ge(s, v)

                def chunk(j, jslot, last, first=False):
                    pe.wait_ge(lo_done, 4 * j + 4 * (c0 + 1))
                    pe.wait_ge(st_lo_done, j + (st0 + 1))
                    _, hi, lo = by_rows((c0 + jslot) % 2)
                    js = jslot % 2
                    for t in range(T):
                        tok = slice(P * t, P * t + P)
                        for k in range(RB):
                            for half in range(2):
                                col = slice(512 * half, 512 * half + 512)
                                bank = ps[:, 2 * t + half, :]
                                pe.matmul(bank, st_hi[:, js, k, tok], hi[:, k, col], start=first and k == 0, stop=False,
                                          skip_group_check=True)
                                pe.matmul(bank, st_hi[:, js, k, tok], lo[:, k, col], start=False, stop=False,
                                          skip_group_check=True)
                                mm = pe.matmul(bank, st_lo[:, js, k, tok], hi[:, k, col], start=False,
                                               stop=last and k == RB - 1, skip_group_check=True)
                        mm.then_inc(products_done, 1)

                chunk(0, 0, n == 1, first=True)
                over_chunks(pe, n, chunk, start=1)

            def up_products(c0, norms, gate_read, gate0, hid0, up_read=None):
                pe.wait_ge(h_lo_done, T * norms)

                def pair(i, first):
                    for which in range(2):
                        pe.wait_ge(lo_done, 8 * i + 4 * (c0 + which + 1))
                        for m in range(2):
                            if not first:
                                if which == 0:
                                    pe.wait_ge(gate_read, 2 * i + (gate0 + m - 1))
                                else:
                                    pe.wait_ge(hid_done, 2 * i + (hid0 + m - 1))
                            turned_projection(2 * which + m, m, (c0 + which) % 2).then_inc(products_done, 1)

                pair(0, True)
                with pe.Fori(1, N_UP // 2) as i:
                    pair(i, False)

            pe.wait_ge(constants_set, 1)
            norm(0)
            mixer(mixers[0])
            row_products(N_OUT, C_OUT1, 0, [(biased, n1.n["unit"]), (probT_done, n1.n["unit"]),
                                            (o_done, n1.n["unit"]), (slot_read, n1.n["turn"]),
                                            (bank_read, n1.n["bank"])])
            norm(1)
            up_products(C_UP1, 2, gate_silu, 0, 0)
            row_products(N_DOWN, C_DOWN1, N_OUT, [(hid_done, MT), (gate_silu, MT)])
            norm(2)
            mixer(mixers[1])
            row_products(N_OUT, C_OUT2, N_OUT + N_DOWN, [(biased, n2.n["unit"]), (probT_done, n2.n["unit"]),
                                                         (o_done, n2.n["unit"]), (slot_read, n2.n["turn"]),
                                                         (bank_read, n2.n["bank"])])
            norm(3)
            pe.wait_ge(h_lo_done, 4 * T)
            pe.wait_ge(p_in, 16)
            for t in range(T):
                for k in range(RB):
                    tr = pe.transpose(ps[:, 4 + k, P * t:P * t + P], p_tok[:, t, P * k:P * k + P], ident[:, :])
            tr.then_inc(small_turned, 1)
            pe.wait_ge(conv_in, 32)
            for j in range(4):
                tr = pe.transpose(ps[:, 6, 2 * MT * j:2 * MT * j + 2 * MT], conv_rows[:, j, :],
                                  ident[0:2 * MT, 0:2 * MT])
            tr.then_inc(small_turned, 1)
            up_products(C_UP2, 4, gate_conv, 0, MT)
            row_products(N_DOWN, C_DOWN2, 2 * N_OUT + N_DOWN, [(hid_done, 2 * MT), (pT_done, 1), (conv_cols_done, 1)])
            norm(4)
            row_products(1, C_PP, 2 * (N_OUT + N_DOWN), [(h_lo_done, 5 * T)])
            for j in range(D // CW):
                for t in range(T):
                    n = T * j + t
                    if t == 0:
                        pe.wait_ge(lo_done, 4 * (C_GATE + j + 1))
                    if n < 8:
                        pe.wait_ge(pp_done, n // 2 + 1)
                    else:
                        pe.wait_ge(sig_done, n - 7)
                    projection(n % 8, t, (C_GATE + j) % 2).then_inc(products_done, 1)


_INS = ['x', 'ln_pre_mix', 'w_in', 'w_pool', 'pool_scale', 'w_out', 'ln_post_mix', 'ln_pre_ffn', 'w_gate',
        'w_up', 'w_down', 'ln_post_ffn', 'p_2', 'ln_mix_2', 'w_in_2', 'qk_gain_2', 'lam_params_2', 'subln_gain_2',
        'fgate_bias_2', 'w_out_2', 'ln_ffn_2', 'w_up_2', 'conv_w_2', 'conv_b_2', 'w_down_2', 'ln_ple_2',
        'w_ple_gate_2', 'w_ple_proj_2']


def _constants():
    f32 = np.float32
    q, k = np.arange(P)[:, None], np.arange(S)[None, :] - (S - P)
    dist = q - k
    seen = dist >= 0
    count = (seen & (dist <= 128)).astype(int) + (seen & (dist % 4 == 0)) + (seen & (dist % 16 == 0))
    log_count = np.where(count > 0, np.log(np.maximum(count, 1)), MASKED)
    allowed = (k + S) // HD <= (q + S) // HD
    slopes = [2.0 ** (-8.0 * (h + 1) / 4) for h in range(4)]
    alibi = np.stack([np.where(allowed, -s * np.abs(dist), MASKED) for s in slopes], axis=1)
    freqs = f32(10000.0) ** (-np.arange(HD // 2, dtype=f32) * f32(2.0 / HD))
    ang = (np.arange(S, dtype=f32)[:, None] * freqs[None, :]).reshape(T, P, HD // 2).transpose(1, 0, 2)
    cos, sin = np.cos(ang), np.sin(ang)
    wins = np.array([2, 4, 8, 16]).repeat(HD).reshape(2, P).T[:, :, None]
    return {
        "log_count": log_count.astype(f32),
        "causal": np.where(seen, 0.0, MASKED).astype(f32),
        "alibi": alibi.astype(f32),
        "rope_cos": np.concatenate([cos, cos], axis=-1).astype(f32),
        "rope_sin": np.concatenate([-sin, sin], axis=-1).astype(f32),
        "pool_inv": (f32(1.0) / np.minimum(np.arange(16) + 1, wins)).astype(f32),
    }


def kernel(**inputs):
    import concourse.bacc as _bacc
    from concourse.bass_utils import run_bass_kernel_spmd as _run

    nc = _bacc.Bacc("TRN2", target_bir_lowering=False, num_devices=1)
    given = {name: np.ascontiguousarray(inputs[name]) for name in _INS}
    dist = np.arange(P)[:, None] - (np.arange(S)[None, :] - (S - P))
    rel = np.asarray(inputs["rel_bias_2"])[0]
    given["rel_table"] = np.ascontiguousarray(rel[:, np.clip(dist, -P, P) + P].transpose(1, 0, 2))
    given.update(_constants())
    arrays, A = {}, {}
    for name, a in given.items():
        arrays[f"in_{name}_dram"] = a
        A[name] = nc.dram_tensor(f"in_{name}_dram", a.shape, mybir.dt.from_np(a.dtype), kind="ExternalInput").ap()
    out = nc.dram_tensor("out_0_dram", (1, S, D), F32, kind="ExternalOutput").ap()
    two_blocks_kernel(nc, A, out)
    r = _run(nc, [arrays], core_ids=[0])
    return r.results[0]["out_0_dram"]
```

```python
from contextlib import ExitStack

import numpy as np

import concourse.bass as bass
from concourse import mybir

P = 128
S = 512
T = S // P
D = 1024
KB = D // P
FF = 2816
MT = FF // P
HD = 64
EPS = 1e-6
CW = 256
RB = 2
CHUNK = KB * CW
QUARTER = CHUNK // 4
KIB = 1024
HALF = 256
BIG = 3.0e38
MASKED = -1.0e30

F32 = mybir.dt.float32
F32R = mybir.dt.float32r
ALU = mybir.AluOpType
ACT = mybir.ActivationFunctionType
AX = mybir.AxisListType.X

DIFF_Q1, DIFF_Q2, DIFF_K1, DIFF_K2, DIFF_V = (256 * i for i in range(5))
FOX = 1280
FOX_GATE = FOX + 3 * 384
CHK = FOX_GATE + 6
DIFF_SCALE = 1.0 - 0.2
LAM_INIT = 0.2

LEAD = 3
SECOND_MAP = (3, 1, 2, 0)
NORMED = ("diff_qk", "fox_qk", "chk_qk")
TURNED = ("q", "k") + NORMED


def parts(steps, heads):
    out = []
    for step in steps:
        if step[0] in heads or not out:
            out.append([])
        out[-1].append(step)
    return out


def interleave(attention, filler):
    units, fillers = parts(attention, ("S",)), parts(filler, ("proj", "poolproj", "poolmix"))
    out, done = [], 0
    for n, unit in enumerate(units):
        want = len(fillers) * (n + 1) // len(units)
        out += unit + sum(fillers[done:want], [])
        done = want
    return out + sum(fillers[done:], [])


def attention_steps(units, after):
    out = []
    for n in range(max([len(units) + 3] + [m + 4 for m in after])):
        if 0 <= n - 2 < len(units):
            out.append(("T", units[n - 2]))
        if n < len(units):
            out.append(("S", units[n]))
        if 0 <= n - 3 < len(units):
            out.append(("PV", units[n - 3]))
        out += after.get(n - 3, [])
    return out


def mixer_steps(groups, after, fillers, last_fillers):
    units = [u for maps in groups for m in maps[::2] for t in range(T) for u in ((m, t), (m + 1, SECOND_MAP[t]))]
    main = attention_steps(units, after)
    starts = [main.index(("S", (maps[0], 0))) for maps in groups]
    out = []
    for lo, hi, filler in zip(starts, starts[1:], fillers):
        out += interleave(main[lo:hi - LEAD], filler) + main[hi - LEAD:hi]
    lo, end = starts[-1], main.index(("S", units[-1])) + 2
    cuts = [lo + (end - lo) * n // len(last_fillers) for n in range(len(last_fillers) + 1)]
    for lo, hi, filler in zip(cuts, cuts[1:], last_fillers):
        out += interleave(main[lo:hi], filler)
    t1, pv1 = main.index(("T", units[-1])), main.index(("PV", units[-1]))
    out += main[end:t1] + [("out", 0)] + main[t1:pv1] + [("out", 1)] + main[pv1:pv1 + 1] + [("out", 2)]
    return out + main[pv1 + 1:] + [("out", 3)]


def projection_steps(chunks, ends, extra=None):
    projs = [(c, t) for c in range(len(chunks)) for t in range(T)]
    runs = [[]]
    for n in range(len(projs) + 2):
        new = []
        if n < len(projs):
            new.append(("proj",) + projs[n])
        kind = [chunks[projs[n - j][0]][0] if 0 <= n - j < len(projs) else None for j in range(3)]
        if kind[1] in NORMED:
            new.append(("rows",) + projs[n - 1])
        if kind[0] and kind[0] not in NORMED:
            new.append(("rows",) + projs[n])
        if kind[2] in NORMED:
            new.append(("qkT",) + projs[n - 2])
        if kind[1] in TURNED and kind[1] not in NORMED:
            new.append(("qkT",) + projs[n - 1])
        if kind[0] in NORMED:
            new.append(("sum",) + projs[n])
        new += (extra or {}).get(n, [])
        for step in new:
            runs[-1].append(step)
            last = ends[len(runs) - 1] - 1 if len(runs) <= len(ends) else None
            if step == ("qkT" if last is not None and chunks[last][0] in TURNED else "rows", last, T - 1):
                runs.append([])
    return runs


def block1_plan():
    chunks = []

    for g in range(3):
        v, q, k = ("v", 1792 + CW * g), ("q", 256 + CW * g), ("k", 1024 + CW * g)
        chunks += [v, q, k] if g == 0 else [q, k, v]
    runs = projection_steps(chunks, (3, 6, 9))
    c = len(chunks)
    chunks.append(("pool", 0))
    after = {8 * j + 8: [("mixT", 2 + j)] for j in range(6)}
    pool = [[("poolproj", c, 0)], [("poolproj", c, 1)], [], [], [("poolmix", 0)], [("poolmix", 1), ("out_rows",)], []]
    return chunks, runs[0] + mixer_steps([range(4 * g, 4 * g + 4) for g in range(3)], after, runs[1:], pool)


def block2_plan():
    chunks = []

    six = [("q", h) for h in range(6)] + [("k", h) for h in range(6)]
    chunks += [("diff_v", DIFF_V, None)]
    chunks += [("diff_qk", col, tile) for col, tile in ((DIFF_Q1, 0), (DIFF_K1, 4), (DIFF_Q2, 2), (DIFF_K2, 6))]
    chunks += [("fox_vg", FOX + 1024, None), ("fox_v", FOX + 768, None)]
    chunks += [("fox_qk", FOX + CW * j, six[4 * j:4 * j + 4]) for j in range(3)]
    chunks += [("chk_qk", CHK + CW * j, six[4 * j:4 * j + 4]) for j in range(3)]
    chunks += [("chk_v2", CHK + 896, None), ("chk_v", CHK + 768, None)]
    gates = 6 * T - 1
    runs = projection_steps(chunks, (5, 10, 15),
                            {gates + 1: [("decay_abs",)], gates + 2: [("decay_ln",)], gates + 3: [("decay",)]})

    after = {n: [] for n in range(90)}
    for h in range(4):
        after[8 * h + 7].append(("combine", h))
        after[8 * h + 8].append(("combine_scale", h))
        if h % 2:
            after[8 * h + 9].append(("mixT", h // 2))
    for j in range(6):
        after[32 + 8 * j + 8].append(("mixT", 2 + j))
    after = {n: a for n, a in after.items() if a}
    return chunks, runs[0] + mixer_steps((range(8), range(8, 14), range(14, 20)), after, runs[1:],
                                         [[("out_rows",)], []])


class Counts:

    def __init__(self, steps, base):
        self.of, self.n = {}, dict(base)
        for s in steps:
            self.of[s] = dict(self.n)
            kind = s[0]
            if kind in ("proj", "poolproj", "poolmix"):
                self.n["product"] += 1
                self.n["bank"] += 1
            elif kind in ("qkT", "mixT", "decay"):
                self.n["turn"] += 1
            elif kind == "S":
                self.n["unit"] += 1
            elif kind == "out":
                self.n["product"] += 1


def two_blocks_kernel(nc, A, out):
    chunks1, steps1 = block1_plan()
    chunks2, steps2 = block2_plan()
    n1 = Counts(steps1, dict(product=0, bank=0, turn=0, unit=0))

    N_OUT, N_DOWN, N_UP = D // (RB * P), MT // RB, 2 * (MT // 2)
    C_OUT1 = len(chunks1)
    C_UP1 = C_OUT1 + N_OUT
    C_DOWN1 = C_UP1 + N_UP
    C_MIX2 = C_DOWN1 + N_DOWN
    C_OUT2 = C_MIX2 + len(chunks2)
    C_UP2 = C_OUT2 + N_OUT
    C_DOWN2 = C_UP2 + N_UP
    C_PP = C_DOWN2 + N_DOWN
    C_GATE = C_PP + 1
    C_END = C_GATE + D // CW

    G_OUT1 = n1.n["product"] - T
    G_UP1 = G_OUT1 + T * N_OUT
    G_DOWN1 = G_UP1 + 2 * N_UP
    G_MIX2 = G_DOWN1 + T * N_DOWN
    n2 = Counts(steps2, {**n1.n, "product": G_MIX2})
    G_OUT2 = n2.n["product"] - T
    G_UP2 = G_OUT2 + T * N_OUT
    G_DOWN2 = G_UP2 + 2 * N_UP
    G_PP = G_DOWN2 + T * N_DOWN
    G_GATE = G_PP + T

    class Mixer:
        pass

    mixers = []
    for b, (cnt, steps, chunks, c0, norm) in enumerate(((n1, steps1, chunks1, 0, 0), (n2, steps2, chunks2, C_MIX2, 2))):
        m = Mixer()
        m.b, m.cnt, m.steps, m.chunks, m.c0, m.norm = b, cnt, steps, chunks, c0, norm
        m.c_out, m.st0 = ((C_OUT1, 0), (C_OUT2, N_OUT + N_DOWN))[b]
        m.unit = {s[1]: cnt.of[s]["unit"] for s in steps if s[0] == "S"}
        m.consumed, m.rows, m.last_turn = {}, {}, {}
        for s in steps:
            if s[0] in ("proj", "poolproj"):
                m.consumed[s[1]] = cnt.of[s]["product"] + 1
                if chunks[s[1]][0] in TURNED:
                    m.rows[s[1], s[2]] = len(m.rows)
            if s[0] == "qkT":
                m.last_turn[s[1], s[2]] = cnt.of[s]["turn"] + 1
        m.turn_of_rows = [m.last_turn[k] for k in m.rows]
        mixers.append(m)

    with ExitStack() as ctx:
        def sb(name, shape, dt=F32):
            return ctx.enter_context(nc.sbuf_tensor(name, shape, dt))

        def sem(name):
            return ctx.enter_context(nc.semaphore(name))

        x = sb("x", [P, T, D])
        h_hi = sb("h_hi", [P, KB, S], F32R)
        h_lo = sb("h_lo", [P, KB, S], F32R)
        w_raw = sb("w_raw", [P, 2, CHUNK])
        w_hi = sb("w_hi", [P, 2, CHUNK], F32R)
        w_lo = sb("w_lo", [P, 2, CHUNK], F32R)
        gain_pre = sb("gain_pre", [P, D])
        ident = sb("ident", [P, P])
        tri = sb("tri", [P, P])
        ones = sb("ones", [P, P])
        causal = sb("causal", [P, S])
        conv_cols = sb("conv_cols", [P, 4, 2 * MT])
        scratch = sb("scratch", [P, 2, CW])
        squares = sb("squares", [P, CW])
        y_ss = sb("y_ss", [P, 2 * T])
        y_rs = sb("y_rs", [P, 2 * T])
        x_ss = sb("x_ss", [P, 5 * T])
        x_rs = sb("x_rs", [P, 5 * T])
        den = sb("den", [P, 8])
        neg_max = sb("neg_max", [P, 8])
        rden = sb("rden", [P, 8])
        qk_ss = sb("qk_ss", [P, 2, 4])
        qk_rs = sb("qk_rs", [P, 2, 4])
        half_neg = sb("half_neg", [P, 4])
        gcol = sb("gcol", [P, 8])
        fcol = sb("fcol", [HD + 2, 2])
        lam = sb("lam", [P, 8])
        den_c = sb("den_c", [P, T])
        gate_bias = sb("gate_bias", [P, 6])
        pool_inv = sb("pool_inv", [P, 2, 16])
        pool_gain = sb("pool_gain", [P, 2])
        decay = sb("decay", [P, 2, T, 6])
        augq = sb("augq", [P, T, 6, 2])
        augk = sb("augk", [P, T, 6, 2])
        arena_kib = 98.5
        sb("arena", [P, int(arena_kib * KIB) // 4])
        arena_start = nc.sbuf_base - int(arena_kib * KIB)
        ps = ctx.enter_context(nc.psum_tensor("ps", [P, 8, 512], F32))

        def at(name, kib, shape, dt=F32):
            assert kib * KIB + int(np.prod(shape[1:])) * 4 <= arena_kib * KIB, name
            return nc.alloc_sbuf_tensor_at(name, shape, dt, offset=arena_start + int(kib * KIB))

        hid = at("hid", 0, [P, MT, S])
        st_hi = at("st_hi", 44, [P, 2, RB, S], F32R)
        st_lo = at("st_lo", 52, [P, 2, RB, S], F32R)
        y_scaled = at("y_scaled", 60, [P, 2, D])
        h_tok = at("h_tok", 68, [P, 2, D])
        junk = at("junk", 76, [P, D])
        act_gate = at("act_gate", 80, [P, 2, S])
        act_val = at("act_val", 84, [P, 2, S])
        p_tok = at("p_tok", 88, [P, T, 256])
        pT = at("pT", 92, [P, RB, S])
        conv_rows = at("conv_rows", 96, [2 * MT, 4, P])
        pp = at("pp", 0, [P, T, D])
        sig = at("sig", 16, [P, 2, CW])
        gain_post = at("gain_post", 94.5, [P, D])
        out_hi = at("out_hi", 86.5, [P, RB, S], F32R)
        out_lo = at("out_lo", 90.5, [P, RB, S], F32R)
        mixT = at("mixT", 0, [P, KB, S])
        qk1 = at("qk1", 16, [P, 2, 4, S])
        v1 = at("v1", 32, [P, 2, T, CW])
        prob1 = at("prob1", 40, [P, 3, S])
        probT1 = at("probT1", 46, [P, 2, S])
        work1 = at("work1", 50, [P, 2, 4 * (HD + 2)])
        otok1 = at("otok1", 55, [P, 2, T, P])
        pool_d = at("pool_d", 60, [P, 2, S])
        pool_u = at("pool_u", 64, [P, 2, S])
        pool_a = at("pool_a", 68, [P, S])
        pool_b = at("pool_b", 70, [P, S])
        log_count = at("log_count", 80, [P, S])
        rope_cos = at("rope_cos", 82, [P, T, HD])
        rope_sin = at("rope_sin", 83, [P, T, HD])
        pool_w = at("pool_w", 84, [P, 2, P])
        lam_in = at("lam_in", 85, [P, 2, 2, HD])
        lam_prod = at("lam_prod", 86, [P, 2, HD])
        qa = at("qa", 16, [P, 8, S])
        va = at("va", 32, [P, T, 384])
        prob2 = at("prob2", 38, [P, 3, S])
        probT2 = at("probT2", 44, [P, 2, S])
        work2 = at("work2", 48, [P, 2, 4 * (HD + 2)])
        otok2 = at("otok2", 50.5, [P, 2, T, P])
        od = at("od", 54.5, [P, T, P])
        table = at("table", 56.5, [P, 6, S])
        fx = at("fx", 68.5, [HD + 2, 12, S])
        vx = at("vx", 92.5, [P, T, 384])

        x_in = [sem(f"x_in{t}") for t in range(T)]
        gain_in = [sem(f"gain_in{n}") for n in range(7)]
        const_in = sem("const_in")
        heads_in = sem("heads_in")
        table_in = sem("table_in")
        bias_in = sem("bias_in")
        conv_in = sem("conv_in")
        p_in = sem("p_in")
        out_in_dram = sem("out_in_dram")
        raw_in = [sem("raw_in0"), sem("raw_in1")]
        hi_done = sem("hi_done")
        lo_done = sem("lo_done")
        products_done = sem("products_done")
        constants_set = sem("constants_set")
        y_squared = sem("y_squared")
        y_rstd = sem("y_rstd")
        y_scaled_done = sem("y_scaled_done")
        x_added = sem("x_added")
        y_gained = sem("y_gained")
        x_half_added = sem("x_half_added")
        x_squared = sem("x_squared")
        x_rstd = sem("x_rstd")
        h_tok_done = sem("h_tok_done")
        h_turned = sem("h_turned")
        h_hi_done = sem("h_hi_done")
        h_lo_done = sem("h_lo_done")
        pool_chain = sem("pool_chain")
        dve_chain = sem("dve_chain")
        bank_read = sem("bank_read")
        sq_done = sem("sq_done")
        ss_done = sem("ss_done")
        rs_done = sem("rs_done")
        turned = sem("turned")
        slot_read = sem("slot_read")
        scores_done = sem("scores_done")
        biased = sem("biased")
        exp_done = sem("exp_done")
        prob_turned = sem("prob_turned")
        probT_done = sem("probT_done")
        pv_done = sem("pv_done")
        o_done = sem("o_done")
        combine_ss = sem("combine_ss")
        combine_rs = sem("combine_rs")
        combined = sem("combined")
        decay_in = sem("decay_in")
        decay_exp = sem("decay_exp")
        decay_sum = sem("decay_sum")
        decay_ln = sem("decay_ln")
        decay_log = sem("decay_log")
        lam_sum = sem("lam_sum")
        lam_exp = sem("lam_exp")
        pool_out = sem("pool_out")
        bias_masked = sem("bias_masked")
        st_hi_done = sem("st_hi_done")
        st_lo_done = sem("st_lo_done")
        gate_silu = sem("gate_silu")
        gate_tap = sem("gate_tap")
        gate_conv = sem("gate_conv")
        val_tap = sem("val_tap")
        hid_done = sem("hid_done")
        tap_chain = sem("tap_chain")
        small_turned = sem("small_turned")
        pT_done = sem("pT_done")
        conv_cols_done = sem("conv_cols_done")
        pp_done = sem("pp_done")
        sig_done = sem("sig_done")
        final_done = sem("final_done")
        N_CONST, N_HEADS = 12, 5

        def by_cols(slot):
            return [w[:, slot, :].rearrange("p (k n) -> p k n", k=KB) for w in (w_raw, w_hi, w_lo)]

        def by_rows(slot):
            return [w[:, slot, :].rearrange("p (k n) -> p k n", k=RB) for w in (w_raw, w_hi, w_lo)]

        def map_operands(b, m):
            low = HD * (m % 2)
            if b == 0:
                g, j, hh = m // 4 % 2, m % 4 // 2, m % 4
                return (qk1[low:low + HD, g, j, :], qk1[low:low + HD, g, 2 + j, :],
                        v1[:, g, :, HD * hh:HD * hh + HD], log_count)
            if m < 8:
                h, w = m // 2, m % 2
                low = HD * (h % 2)
                return (qa[low:low + HD, 2 * w + h // 2, :], qa[low:low + HD, 4 + 2 * w + h // 2, :],
                        va[:, :, HD * h:HD * h + HD], table[:, h, :])
            if m < 14:
                h = m - 8
                return fx[:, h, :], fx[:, 6 + h, :], vx[:, :, HD * h:HD * h + HD], causal
            h = m - 14
            return (qa[low:low + HD, h // 2, :], qa[low:low + HD, 3 + h // 2, :],
                    va[:, :, HD * h:HD * h + HD], table[:, h, :])

        def group_of(b, m):
            if b == 0:
                return [3 * (m // 4) + j for j in range(3)]
            kinds = ("diff_v", "diff_qk") if m < 8 else ("fox_vg", "fox_v", "fox_qk") if m < 14 else \
                ("chk_v2", "chk_v", "chk_qk")
            return [c for c, ch in enumerate(chunks2) if ch[0] in kinds]

        def rows_turned(mx, m):
            return max(mx.cnt.of[s]["turn"] + 1 for s in mx.steps if s[0] == "qkT" and s[1] in group_of(mx.b, m))

        def values_read(mx, m):
            return max(mx.cnt.of[s]["bank"] + 1 for s in mx.steps if s[0] == "proj" and s[1] in group_of(mx.b, m))

        def row_source(b, kb):
            if b == 0:
                pair = kb - 2
                return otok1[:, pair % 2, :, :], (2 * pair + 1, 0)
            if kb < 2:
                return od[:, :, :], None
            pair = kb + 2
            return otok2[:, pair % 2, :, :], (2 * pair + 1, 0)

        def turned_rows(t):
            return ps[:, 2 * t:2 * t + 2, :].rearrange("p a (k n) -> p (a k) n", n=P)

        def over_chunks(eng, n, chunk, start=0):
            pairs = max(0, (n - 1 - start) // 2)
            if pairs > 1:
                with eng.Fori(0, pairs) as i:
                    for s in range(2):
                        chunk(2 * i + (start + s), start + s, False)
            else:
                pairs = 0
            for j in range(start + 2 * pairs, n):
                chunk(j, j, j == n - 1)

        block = ctx.enter_context(nc.Block())

        @block.sync
        def _(sp):
            def load(c, slot, src, rows=False, first=False):
                if not first:
                    sp.wait_ge(lo_done, 4 * (c - 1))
                dst = (by_rows if rows else by_cols)(slot)[0]
                sp.dma_start(dst, src).then_inc(raw_in[slot], 16)

            def cols(w, col):
                return w.rearrange("(k p) n -> p k n", p=P)[:, :, bass.ds(col, CW)]

            def rows(w):
                return w.rearrange("(j k p) n -> j p k n", p=P, k=RB)

            def row_chunks(w, c0):
                n = w.shape[0] // (RB * P)
                odd = n % 2
                if odd:
                    load(c0, c0 % 2, rows(w)[0], rows=True)
                with sp.Fori(0, n // 2) as i:
                    for s in range(2):
                        load(2 * i + (c0 + odd + s), (c0 + odd + s) % 2, rows(w)[2 * i + (odd + s)], rows=True)

            def column_pairs(gate, up, off, c0):
                with sp.Fori(0, N_UP // 2) as i:
                    load(2 * i + c0, c0 % 2, cols(gate, CW * i))
                    load(2 * i + (c0 + 1), (c0 + 1) % 2, cols(up, CW * i + off))

            def const(dst, src, **kw):
                sp.dma_start(dst, src, **kw).then_inc(const_in, 16)

            def bcast(a, n):
                return bass.AP(a.tensor, a.offset, [[0, P], [1, n]])

            for t in range(T):
                sp.dma_start(x[:, t, :], A["x"][0, P * t:P * t + P, :]).then_inc(x_in[t], 16)
                if t == 0:
                    sp.dma_start(gain_pre[:, :], bcast(A["ln_pre_mix"], D)).then_inc(gain_in[0], 16)
                if t == 1:
                    load(0, 0, cols(A["w_in"][0], chunks1[0][1]), first=True)
            const(rope_cos[:, :, :], A["rope_cos"])
            const(rope_sin[:, :, :], A["rope_sin"])
            load(1, 1, cols(A["w_in"][0], chunks1[1][1]), first=True)
            const(log_count[:, :], A["log_count"])
            const(causal[:, :], A["causal"])
            const(lam_in[:, :, :, :], bcast(A["lam_params_2"], 4 * HD).rearrange("p (a b d) -> p a b d", a=2, b=2))
            for half in range(2):
                feat = slice(HD * half, HD * half + HD)
                const(gcol[feat, 0:6], A["qk_gain_2"][0].rearrange("n d -> d n"), allow_slow_non_contiguous=True)
                const(gcol[feat, 6:7], A["subln_gain_2"].rearrange("n d -> d n"), allow_slow_non_contiguous=True)
            const(gate_bias[:, :], bcast(A["fgate_bias_2"], 6))
            const(pool_inv[:, :, :], A["pool_inv"])
            const(pool_gain[:, :], A["pool_scale"][0].rearrange("(m p) -> p m", p=P), allow_slow_non_contiguous=True)
            for c, (kind, col) in enumerate(chunks1):
                if c >= 2:
                    load(c, c % 2, cols(A["w_in"][0], col))
            row_chunks(A["w_out"][0], C_OUT1)
            column_pairs(A["w_gate"][0], A["w_up"][0], 0, C_UP1)
            row_chunks(A["w_down"][0], C_DOWN1)
            for j, (kind, col, _) in enumerate(chunks2):
                load(C_MIX2 + j, (C_MIX2 + j) % 2, cols(A["w_in_2"][0], col))
            row_chunks(A["w_out_2"][0], C_OUT2)
            column_pairs(A["w_up_2"][0], A["w_up_2"][0], FF, C_UP2)
            row_chunks(A["w_down_2"][0], C_DOWN2)
            load(C_PP, C_PP % 2, rows(A["w_ple_proj_2"][0])[0], rows=True)
            for j in range(D // CW):
                load(C_GATE + j, (C_GATE + j) % 2, cols(A["w_ple_gate_2"][0], CW * j))
            o = out[0].rearrange("(t p) n -> t p n", p=P)
            for j in range(D // CW):
                for t in range(T):
                    sp.wait_ge(final_done, T * j + t + 1)
                    sp.dma_start(o[t, :, CW * j:CW * j + CW], x[:, t, CW * j:CW * j + CW]).then_inc(out_in_dram, 16)
            sp.wait_ge(out_in_dram, 16 * T * (D // CW))

        @block.gpsimd
        def _(pool):
            chain = [0]

            def link(ins):
                chain[0] += 1
                ins.then_inc(pool_chain, 1)
                pool.wait_ge(pool_chain, chain[0])

            def rstd(out_, ss, n, width):
                link(pool.tensor_scalar(ss, ss, 1.0 / width, EPS, ALU.mult, ALU.add))
                return pool.tensor_tensor(out_, ss, half_neg[:, 0:n], ALU.pow)

            def gain(n, dst, name):
                a = A[name]
                pool.dma_start(dst, bass.AP(a.tensor, a.offset, [[0, P], [1, D]])).then_inc(gain_in[n], 16)

            link(pool.memset(half_neg[:, :], -0.5))
            link(pool.memset(ident[:, :], 0.0))
            pool.affine_select(out=ident[:, :], in_=ident[:, :], compare_op=ALU.not_equal, fill=1.0,
                                    base=0, pattern=[[-1, P]], channel_multiplier=1).then_inc(constants_set, 1)

            def norm(b, post):
                for s in range(T + 1):
                    if s < T and post:
                        n = T * (b - 1) + s
                        pool.wait_ge(y_squared, n + 1)
                        rstd(y_rs[:, n:n + 1], y_ss[:, n:n + 1], 1, D).then_inc(y_rstd, 1)
                    if s >= 1:
                        n = T * b + s - 1
                        pool.wait_ge(x_squared, n + 1)
                        rstd(x_rs[:, n:n + 1], x_ss[:, n:n + 1], 1, D).then_inc(x_rstd, 1)
                    if s < T and post:
                        n = T * (b - 1) + s
                        pool.wait_ge(y_scaled_done, n + 1)
                        pool.tensor_tensor(x[:, s, 0:HALF], x[:, s, 0:HALF], y_scaled[:, n % 2, 0:HALF], ALU.add)\
                            .then_inc(x_half_added, 1)

            def mixer(mx):
                for s in mx.steps:
                    kind = s[0]
                    if kind == "sum":
                        r = mx.rows[s[1], s[2]]
                        pool.wait_ge(ss_done, r + 1)
                        rstd(qk_rs[:, r % 2, :], qk_ss[:, r % 2, :], 4, HD).then_inc(rs_done, 1)
                    if kind == "proj" and mx.b == 1 and mx.chunks[s[1]][0] == "chk_v2" and s[2] == 0:
                        pool.wait_ge(biased, mx.unit[7, 0] + 1)
                        pool.dma_start(table[:, :, :], A["rel_table"]).then_inc(bias_in, 16)
                    if kind == "proj" and mx.b == 1 and mx.chunks[s[1]][0] == "chk_v" and s[2] == 0:
                        pool.wait_ge(bias_in, 16)
                        pool.memset(table[0:HD, :, S - HD:S], MASKED).then_inc(bias_masked, 1)
                    if kind == "combine":
                        pool.wait_ge(combine_ss, s[1] + 1)
                        rstd(lam[:, 4:8], den_c[:, :], 4, HD).then_inc(combine_rs, 1)
                    if kind == "poolproj":
                        window_means(s[2], mx.cnt.of[s]["bank"] + 1)

            def window_means(m, copied):
                u, d, a, b = pool_u[:, m, :], pool_d[:, m, :], pool_a, pool_b
                pool.wait_ge(bank_read, copied)

                def widen(dst, src, sh):
                    link(pool.tensor_copy(dst[:, 0:sh], src[:, 0:sh]))
                    link(pool.tensor_tensor(dst[:, sh:S], src[:, sh:S], src[:, 0:S - sh], ALU.add))

                widen(a[:, :], u, 1)
                widen(b[:, :], a[:, :], 2)
                if m:
                    widen(a[:, :], b[:, :], 4)
                    widen(b[:, :], a[:, :], 8)
                for half, src in ((0, a), (1, b)):
                    lo = HD * half
                    win = 2 << (2 * m + half)
                    link(pool.tensor_scalar(d[lo:lo + HD], src[lo:lo + HD, :], 1.0 / win, None, ALU.mult))
                    link(pool.tensor_tensor(d[lo:lo + HD, 0:16], src[lo:lo + HD, 0:16],
                                            pool_inv[lo:lo + HD, m, :], ALU.mult))
                pool.tensor_tensor(d, d, u, ALU.subtract).then_inc(pool_out, 1)

            norm(0, False)
            pool.memset(ones[:, :], 1.0)
            link(pool.memset(tri[:, :], 1.0))
            link(pool.affine_select(out=tri[:, :], in_=tri[:, :], compare_op=ALU.is_ge, fill=0.0,
                                    base=0, pattern=[[1, P]], channel_multiplier=-1))
            link(pool.memset(augq[:, :, :, 1], 1.0))
            link(pool.memset(augk[:, :, :, 0], 1.0))
            link(pool.memset(fcol[:, :], 1.0))
            pool.memset(pool_w[:, :, :], 0.0).then_inc(constants_set, 1)
            pool.wait_ge(constants_set, 2)
            for g in range(4):
                low = HD * (g % 2)
                pool.dma_start(pool_w[low:low + HD, g // 2, low:low + HD], A["w_pool"][0, g]).then_inc(heads_in, 16)
            pool.dma_start(fcol[0:HD, :], A["qk_gain_2"][0, 2:4].rearrange("n d -> d n"),
                           allow_slow_non_contiguous=True).then_inc(heads_in, 16)
            pool.wait_ge(const_in, 16 * N_CONST)
            mixer(mixers[0])
            gain(1, gain_post[:, :], "ln_post_mix")
            pool.wait_ge(h_tok_done, T)
            gain(2, gain_pre[:, :], "ln_pre_ffn")
            norm(1, True)
            pool.wait_ge(h_tok_done, 2 * T)
            gain(3, gain_post[:, :], "ln_post_ffn")
            gain(4, gain_pre[:, :], "ln_mix_2")
            norm(2, True)
            pool.wait_ge(h_lo_done, 3 * T)
            gain(5, gain_pre[:, :], "ln_ffn_2")
            pool.dma_start(table[:, 0:4, :], A["alibi"]).then_inc(table_in, 16)
            mixer(mixers[1])
            pool.wait_ge(products_done, G_OUT2 + T)
            pool.dma_start(conv_rows[:, 0:3, :], A["conv_w_2"][0].rearrange("j (m q) -> m j q", q=P))\
                .then_inc(conv_in, 16)
            pool.dma_start(conv_rows[:, 3, :], A["conv_b_2"][0].rearrange("(m q) -> m q", q=P)).then_inc(conv_in, 16)
            pool.dma_start(p_tok[:, :, :], A["p_2"][0, 0].rearrange("(t p) n -> p t n", p=P)).then_inc(p_in, 16)
            norm(3, False)
            pool.wait_ge(h_lo_done, 4 * T)
            gain(6, gain_pre[:, :], "ln_ple_2")
            norm(4, False)

        @block.scalar
        def _(act):
            def split_hi(c, slot, quarter, free):
                if quarter == 0:
                    act.wait_ge(raw_in[slot], 8 * c + (16 - 8 * slot))
                    if free is not None:
                        act.wait_ge(products_done, free)
                q = slice(QUARTER * quarter, QUARTER * quarter + QUARTER)
                act.activation(w_hi[:, slot, q], w_raw[:, slot, q], ACT.Copy).then_inc(hi_done, 1)

            def norm(b, post, g_y, between=None):
                def junk_free(ys, xs):
                    if ys > 0:
                        act.wait_ge(y_squared, ys)
                    if xs > 0:
                        act.wait_ge(x_squared, xs)

                ys0 = T * (b - 1) if post else T * min(b - 1, 2)
                for s in range(T + 2):
                    if s < T and post:
                        n = T * (b - 1) + s
                        act.wait_ge(products_done, g_y + s + 1)
                        junk_free(n, T * b + max(s - 1, 0))
                        act.activation(junk[:, :], ps[:, 2 * s:2 * s + 2, :].rearrange("p a n -> p (a n)"),
                                       ACT.Square, accum_out=y_ss[:, n:n + 1]).then_inc(y_squared, 1)
                    if 1 <= s <= T:
                        n = T * b + s - 1
                        if b == 0:
                            act.wait_ge(x_in[s - 1], 16)
                        else:
                            act.wait_ge(x_added, n - T + 1)
                            if post:
                                act.wait_ge(x_half_added, n - T + 1)
                        junk_free(ys0 + (min(s + 1, T) if post else 0), n)
                        act.activation(junk[:, :], x[:, s - 1, :], ACT.Square, accum_out=x_ss[:, n:n + 1])\
                            .then_inc(x_squared, 1)
                    if s >= 2:
                        t = s - 2
                        act.wait_ge(h_turned, T * b + t + 1)
                        act.activation(h_hi[:, :, P * t:P * t + P], turned_rows(t), ACT.Copy).then_inc(h_hi_done, 1)
                    if between:
                        between(s)

            def mixer(mx):
                for s in mx.steps:
                    kind, of = s[0], mx.cnt.of[s]
                    if kind in ("proj", "poolproj"):
                        c = mx.c0 + s[1] + 1
                        free = mx.consumed[s[1] - 1] if s[1] else (G_MIX2 if mx.b else None)
                        for q in ([s[2]] if kind == "proj" else [2 * s[2], 2 * s[2] + 1]):
                            split_hi(c, c % 2, q, free)
                    if kind == "proj" and mx.b == 1 and (s[1], s[2]) in mx.rows:
                        r = mx.rows[s[1], s[2]]
                        act.wait_ge(products_done, of["product"] + 1)
                        if r >= 2:
                            act.wait_ge(ss_done, r - 1)
                        act.activation(scratch[:, r % 2, :], ps[:, of["bank"] % 2, 0:CW], ACT.Square)\
                            .then_inc(sq_done, 1)
                    if kind == "S":
                        u, kn = mx.unit[s[1]], P * (s[1][1] + 1)
                        prob = (prob1, prob2)[mx.b][:, u % 3, 0:kn]
                        act.wait_ge(biased, u + 1)
                        act.activation(prob, prob, ACT.Exp, bias=neg_max[:, u % 8:u % 8 + 1], scale=-1.0,
                                       accum_out=den[:, u % 8:u % 8 + 1]).then_inc(exp_done, 1)
                    if kind == "T":
                        u, kn = mx.unit[s[1]], P * (s[1][1] + 1)
                        act.wait_ge(prob_turned, u + 1)
                        if u >= 2:
                            act.wait_ge(pv_done, u - 1)
                        act.activation((probT1, probT2)[mx.b][:, u % 2, 0:kn], ps[:, 4 + u % 2, 0:kn], ACT.Copy)\
                            .then_inc(probT_done, 1)
                    if kind == "out":
                        c = mx.c_out + 1
                        split_hi(c, c % 2, s[1], mx.consumed[len(mx.chunks) - 1])
                    if kind == "out_rows":
                        if mx.b == 0:
                            act.wait_ge(bank_read, of["bank"])
                        else:
                            act.wait_ge(slot_read, mx.cnt.of["mixT", 1]["turn"] + 1)
                            act.wait_ge(pv_done, mx.unit[13, 0] + 1)
                        act.activation(out_hi[:, :, :], mixT[:, 0:RB, :], ACT.Copy).then_inc(st_hi_done, 1)
                    if kind == "decay_abs":
                        act.wait_ge(decay_in, 1)
                        act.activation(decay[:, 1, :, :], decay[:, 1, :, :], ACT.Exp).then_inc(decay_exp, 1)
                    if kind == "decay_ln":
                        act.wait_ge(decay_sum, 1)
                        act.activation(decay[:, 1, :, :], decay[:, 1, :, :], ACT.Ln).then_inc(decay_ln, 1)

            def row_products(src, n, c0, g0, st0, ready, start=0):
                def rows_hi(j, slot):
                    act.activation(st_hi[:, slot, :, :], src[:, bass.ds(2 * j, RB), :], ACT.Copy).then_inc(st_hi_done, 1)

                def chunk(j, jslot, last):
                    for t in range(T):
                        slot = (c0 + jslot + 1) % 2
                        split_hi(c0 + j + 1, slot, t, g0 + T * j)
                        if t == 0 and not last:
                            rows_hi(j + 1, (jslot + 1) % 2)

                if start == 0:
                    for t in range(T):
                        split_hi(c0 + 1, (c0 + 1) % 2, t, g0)
                for s, v in ready:
                    act.wait_ge(s, v)
                rows_hi(1, 1)
                over_chunks(act, n, chunk, start=1)

            def first_rows_hi():
                act.activation(st_hi[:, 0, :, :], hid[:, 0:RB, :], ACT.Copy).then_inc(st_hi_done, 1)

            def swiglu(c0, g0):
                def pair(i, first=False, last=False):
                    if last:
                        first_rows_hi()
                    for m in range(2):
                        for q in (2 * m, 2 * m + 1):
                            split_hi(2 * i + (c0 + 1), (c0 + 1) % 2, q, 4 * i + g0)
                        act.wait_ge(products_done, 4 * i + (g0 + m + 1))
                        if not first:
                            act.wait_ge(hid_done, 2 * i + (m - 1))
                        act.activation(act_gate[:, m, :], ps[:, m, :], ACT.Silu).then_inc(gate_silu, 1)
                    for q in range(4):
                        split_hi(2 * i + (c0 + 2), c0 % 2, q, 4 * i + (g0 + 2))

                pair(0, first=True)
                with act.Fori(1, N_UP // 2 - 1) as i:
                    pair(i)
                pair(N_UP // 2 - 1, last=True)

            def conv_swiglu(c0, g0, hid0):
                def tap(dst, m, src, col, sem_):
                    act.activation(dst[:, m, :], src, ACT.Identity, bias=conv_cols[:, 3, bass.ds(col, 1)],
                                   scale=conv_cols[:, 2, bass.ds(col, 1)]).then_inc(sem_, 1)

                def pair(i, first=False, last=False):
                    if last:
                        first_rows_hi()
                    for q in range(4):
                        split_hi(2 * i + (c0 + 1), (c0 + 1) % 2, q, 4 * i + g0)
                    if first:
                        act.wait_ge(small_turned, 1)
                        act.activation(pT[:, :, :], ps[:, 4:6, :], ACT.Copy).then_inc(pT_done, 1)
                        act.wait_ge(conv_cols_done, 1)
                    for m in range(2):
                        act.wait_ge(products_done, 4 * i + (g0 + m + 1))
                        if not first:
                            act.wait_ge(hid_done, 2 * i + (hid0 + m - 1))
                        tap(act_gate, m, ps[:, m, :], 2 * i + m, gate_tap)
                    for q in range(4):
                        split_hi(2 * i + (c0 + 2), c0 % 2, q, 4 * i + (g0 + 2))
                    for m in range(2):
                        act.wait_ge(gate_conv, 2 * i + (m + 1))
                        act.activation(act_gate[:, m, :], act_gate[:, m, :], ACT.Silu).then_inc(gate_silu, 1)
                    for m in range(2):
                        act.wait_ge(products_done, 4 * i + (g0 + m + 3))
                        tap(act_val, m, ps[:, 2 + m, :], 2 * i + (MT + m), val_tap)

                pair(0, first=True)
                with act.Fori(1, N_UP // 2 - 1) as i:
                    pair(i)
                pair(N_UP // 2 - 1, last=True)

            def first_weights(s):
                if s == 2:
                    for q in range(4):
                        split_hi(0, 0, q, None)

            norm(0, False, 0, first_weights)
            mixer(mixers[0])
            act.wait_ge(lam_sum, 1)
            act.activation(lam[:, 2:4], lam[:, 0:2], ACT.Exp).then_inc(lam_exp, 1)
            row_products(mixT, N_OUT, C_OUT1, G_OUT1, 0,
                         [(slot_read, n1.n["turn"]), (bank_read, n1.n["bank"]), (products_done, G_OUT1 + 2)], start=1)
            norm(1, True, G_UP1 - T)
            swiglu(C_UP1, G_UP1)
            row_products(hid, N_DOWN, C_DOWN1, G_DOWN1, N_OUT, [(hid_done, MT)])
            norm(2, True, G_MIX2 - T)
            mixer(mixers[1])
            row_products(mixT, N_OUT, C_OUT2, G_OUT2, N_OUT + N_DOWN,
                         [(slot_read, n2.n["turn"]), (bank_read, n2.n["bank"]), (products_done, G_OUT2 + 2)], start=1)
            norm(3, False, G_UP2 - T)
            conv_swiglu(C_UP2, G_UP2, MT)
            row_products(hid, N_DOWN, C_DOWN2, G_DOWN2, 2 * N_OUT + N_DOWN, [(hid_done, 2 * MT)])
            act.wait_ge(products_done, G_PP - T)
            act.activation(st_hi[:, 1, :, :], pT[:, :, :], ACT.Copy).then_inc(st_hi_done, 1)

            def gate_weights(s):
                if 1 <= s <= T:
                    split_hi(C_GATE, C_GATE % 2, s - 1, G_PP)

            norm(4, False, G_PP - T, gate_weights)
            for t in range(T):
                act.wait_ge(products_done, G_PP + t + 1)
                act.activation(pp[:, t, :], ps[:, 2 * t:2 * t + 2, :].rearrange("p a n -> p (a n)"), ACT.Copy)\
                    .then_inc(pp_done, 1)
            for j in range(D // CW):
                for t in range(T):
                    n = T * j + t
                    if j + 1 < D // CW:
                        split_hi(C_GATE + j + 1, (C_GATE + j + 1) % 2, t, G_GATE + T * j)
                    act.wait_ge(products_done, G_GATE + n + 1)
                    if n >= 2:
                        act.wait_ge(final_done, n - 1)
                    act.activation(sig[:, n % 2, :], ps[:, n % 8, 0:CW], ACT.Sigmoid).then_inc(sig_done, 1)

        @block.vector
        def _(dve):
            chain = [0]

            def link(ins):
                chain[0] += 1
                ins.then_inc(dve_chain, 1)
                dve.wait_ge(dve_chain, chain[0])

            def split_lo(c, slot, quarter):
                dve.wait_ge(hi_done, 4 * c + (quarter + 1))
                q = slice(QUARTER * quarter, QUARTER * quarter + QUARTER)
                dve.tensor_tensor(w_lo[:, slot, q], w_raw[:, slot, q], w_hi[:, slot, q].bitcast(F32), ALU.subtract).then_inc(lo_done, 1)

            def norm(b, post, g_y, between=None):
                for s in range(T + 2):
                    if s < T and post:
                        n = T * (b - 1) + s
                        dve.wait_ge(y_squared, n + 1)
                        if s == 0:
                            dve.wait_ge(gain_in[2 * b - 1], 16)
                        if n >= 2:
                            dve.wait_ge(x_half_added, n - 1)
                        y = ps[:, 2 * s:2 * s + 2, :].rearrange("p a n -> p (a n)")
                        scaled, rest = y_scaled[:, n % 2, 0:HALF], y_scaled[:, n % 2, HALF:D]
                        dve.tensor_tensor(rest, y[:, HALF:D], gain_post[:, HALF:D], ALU.mult).then_inc(y_gained, 1)
                        dve.wait_ge(y_rstd, n + 1)
                        dve.scalar_tensor_tensor(out=scaled, in0=y[:, 0:HALF], scalar=y_rs[:, n:n + 1],
                                                 in1=gain_post[:, 0:HALF], op0=ALU.mult, op1=ALU.mult)\
                            .then_inc(y_scaled_done, 1)
                        dve.wait_ge(y_gained, n + 1)
                        dve.scalar_tensor_tensor(out=x[:, s, HALF:D], in0=rest, scalar=y_rs[:, n:n + 1],
                                                 in1=x[:, s, HALF:D], op0=ALU.mult, op1=ALU.add).then_inc(x_added, 1)
                    if s < T and b >= 3:
                        dve.wait_ge(products_done, g_y + s + 1)
                        dve.tensor_tensor(x[:, s, :], x[:, s, :],
                                          ps[:, 2 * s:2 * s + 2, :].rearrange("p a n -> p (a n)"), ALU.add)\
                            .then_inc(x_added, 1)
                    if 1 <= s <= T:
                        n = T * b + s - 1
                        dve.wait_ge(x_rstd, n + 1)
                        if s == 1:
                            dve.wait_ge(gain_in[(0, 2, 4, 5, 6)[b]], 16)
                        if n >= 2:
                            dve.wait_ge(h_turned, n - 1)
                        dve.scalar_tensor_tensor(out=h_tok[:, n % 2, :], in0=x[:, s - 1, :],
                                                 scalar=x_rs[:, n:n + 1], in1=gain_pre[:, :],
                                                 op0=ALU.mult, op1=ALU.mult).then_inc(h_tok_done, 1)
                    if s >= 2:
                        t = s - 2
                        dve.wait_ge(h_hi_done, T * b + t + 1)
                        dve.tensor_tensor(h_lo[:, :, P * t:P * t + P], turned_rows(t),
                                          h_hi[:, :, P * t:P * t + P].bitcast(F32), ALU.subtract)\
                            .then_inc(h_lo_done, 1)
                    if between:
                        between(s)

            EARLY = (("rows", 0, 0), ("rows", 0, 1))

            def early_rows(mx, s):
                if s >= T:
                    rows_of_projection(mx, EARLY[s - T])

            def heads4(ap):
                return ap.rearrange("p (h d) -> p h d", d=HD)

            def sum_squares(mx, s):
                r = mx.rows[s[1], s[2]]
                dve.wait_ge(sq_done, r + 1)
                if r >= 2:
                    dve.wait_ge(rs_done, r - 1)
                dve.tensor_reduce(qk_ss[:, r % 2, :], heads4(scratch[:, r % 2, :]), AX, ALU.add).then_inc(ss_done, 1)

            def rows_of_projection(mx, s):
                kind, of = mx.chunks[s[1]][0], mx.cnt.of["proj", s[1], s[2]]
                t, bank = s[2], ps[:, of["bank"] % 2, :]
                dve.wait_ge(products_done, of["product"] + 1)
                if (s[1], s[2]) in mx.rows:
                    r = mx.rows[s[1], s[2]]
                    if r >= 2:
                        dve.wait_ge(turned, mx.turn_of_rows[r - 2])
                if (mx.b, s[1], t) == (0, 0, 0):
                    dve.wait_ge(const_in, 16 * N_CONST)
                if kind in ("q", "k"):
                    w = heads4(work1[:, r % 2, 0:CW])
                    sw = heads4(scratch[:, r % 2, :])
                    src = heads4(bank[:, 0:CW])
                    half = HD // 2
                    dve.tensor_tensor(w, src, rope_cos[:, t:t + 1, :].to_broadcast([P, 4, HD]), ALU.mult)
                    dve.tensor_tensor(sw[:, :, 0:half], src[:, :, half:HD],
                                      rope_sin[:, t:t + 1, 0:half].to_broadcast([P, 4, half]), ALU.mult)
                    link(dve.tensor_tensor(sw[:, :, half:HD], src[:, :, 0:half],
                                           rope_sin[:, t:t + 1, half:HD].to_broadcast([P, 4, half]), ALU.mult))
                    dve.tensor_tensor(w, w, sw, ALU.add).then_inc(bank_read, 1)
                elif kind == "v":
                    dve.tensor_copy(v1[:, s[1] // 3 % 2, t, :], bank[:, 0:CW]).then_inc(bank_read, 1)
                elif kind == "chk_v":
                    dve.tensor_copy(va[:, t, 0:P], bank[:, 0:P]).then_inc(bank_read, 1)
                elif kind == "diff_v":
                    dve.tensor_copy(va[:, t, 0:CW], bank[:, 0:CW]).then_inc(bank_read, 1)
                elif kind == "fox_v":
                    dve.tensor_copy(vx[:, t, 0:CW], bank[:, 0:CW]).then_inc(bank_read, 1)
                elif kind == "chk_v2":
                    dve.tensor_copy(va[:, t, P:384], bank[:, 0:CW]).then_inc(bank_read, 1)
                elif kind == "fox_vg":
                    dve.tensor_tensor(decay[:, 0, t, :], bank[:, P:P + 6], gate_bias[:, :], ALU.add)
                    dve.tensor_copy(vx[:, t, CW:384], bank[:, 0:P]).then_inc(bank_read, 1)
                else:
                    if kind == "fox_qk":
                        w = work2[:, r % 2, :].rearrange("p (h d) -> p h d", d=HD + 2)
                        for j in range(2):
                            which, h = mx.chunks[s[1]][2][2 * j]
                            aug = augq if which == "q" else augk
                            dve.tensor_copy(w[:, 2 * j:2 * j + 2, HD:HD + 2], aug[:, t, h:h + 2, :])
                        w = w[:, :, 0:HD]
                    else:
                        w = heads4(work2[:, r % 2, 0:CW])
                    dve.wait_ge(rs_done, r + 1)
                    dve.tensor_tensor(w, heads4(bank[:, 0:CW]),
                                      qk_rs[:, r % 2, :].rearrange("p (h o) -> p h o", o=1).to_broadcast([P, 4, HD]),
                                      ALU.mult).then_inc(bank_read, 1)

            def read_turned(mx, s, of):
                turn = ps[:, 7, :].rearrange("p (j n) -> p j n", n=P)
                dve.wait_ge(turned, of["turn"] + 1)
                if s[0] == "mixT":
                    if mx.b == 1 and s[1] < 2:
                        dve.tensor_scalar(mixT[:, s[1], :], ps[:, 7, :], gcol[:, 6:7], None, ALU.mult)\
                            .then_inc(slot_read, 1)
                    else:
                        dve.tensor_copy(mixT[:, s[1], :], ps[:, 7, :]).then_inc(slot_read, 1)
                    return
                chunk, tok = mx.chunks[s[1]], slice(P * s[2], P * s[2] + P)
                if chunk[0] in ("q", "k"):
                    first = 0 if chunk[0] == "q" else 2
                    dve.tensor_scalar(qk1[:, s[1] // 3 % 2, first:first + 2, tok], turn[:, 0:2, :],
                                      0.125 if first == 0 else 1.0, None, ALU.mult).then_inc(slot_read, 1)
                elif chunk[0] == "diff_qk":
                    g = 0 if chunk[2] < 4 else 1
                    dve.tensor_scalar(qa[:, chunk[2]:chunk[2] + 2, tok], turn[:, 0:2, :],
                                      gcol[:, g:g + 1], None, ALU.mult).then_inc(slot_read, 1)
                elif chunk[0] == "chk_qk":
                    for j in range(2):
                        which, h = chunk[2][2 * j]
                        tile, g = (h // 2, 4) if which == "q" else (3 + h // 2, 5)
                        ins = dve.tensor_scalar(qa[:, tile, tok], turn[:, j, :], gcol[:, g:g + 1], None, ALU.mult)
                    ins.then_inc(slot_read, 1)
                else:
                    for j in range(2):
                        which, h = chunk[2][2 * j]
                        tile, g = (h, 0) if which == "q" else (6 + h, 1)
                        ins = dve.tensor_scalar(fx[:, tile:tile + 2, tok], turn[0:HD + 2, 2 * j:2 * j + 2, :],
                                                fcol[:, g:g + 1], None, ALU.mult)
                    ins.then_inc(slot_read, 1)

            z_gate, e_gate = decay[:, 0, :, :], decay[:, 1, :, :]

            def decay_abs(mx):
                gates = max(mx.cnt.of[s]["bank"] for s in mx.steps if s[0] == "proj" and mx.chunks[s[1]][0] == "fox_vg")
                dve.wait_ge(bank_read, gates + 1)
                dve.scalar_tensor_tensor(out=e_gate, in0=z_gate, scalar=-1.0, in1=z_gate, op0=ALU.mult, op1=ALU.min)\
                    .then_inc(decay_in, 1)

            def decay_rows(of):
                dve.wait_ge(decay_ln, 1)
                dve.scalar_tensor_tensor(out=z_gate, in0=z_gate, scalar=0.0, in1=e_gate, op0=ALU.min, op1=ALU.subtract)\
                    .then_inc(decay_log, 1)
                dve.wait_ge(turned, of["turn"] + 1)
                f = ps[:, 7, 0:6 * T].rearrange("p (t h) -> p t h", t=T)
                dve.tensor_copy(augq[:, :, :, 0], f)
                dve.tensor_scalar(augk[:, :, :, 1], f, -1.0, None, ALU.mult).then_inc(slot_read, 1)
                dve.wait_ge(slot_read, of["turn"] + 1)

            def combine(mx, h):
                o = otok2[:, h % 2, :, :]
                low = HD * (h % 2)
                dst = od[:, :, low:low + HD]
                dve.wait_ge(o_done, mx.unit[2 * h + 1, 0] + 1)
                link(dve.scalar_tensor_tensor(out=dst, in0=o[:, :, HD:P], scalar=lam[:, 2:3], in1=o[:, :, 0:HD],
                                              op0=ALU.mult, op1=ALU.add))
                sq = squares[:, :].rearrange("p (t d) -> p t d", t=T)
                link(dve.tensor_tensor(sq, dst, dst, ALU.mult))
                dve.tensor_reduce(den_c[:, :], sq, AX, ALU.add).then_inc(combine_ss, 1)

            def combine_scale(h):
                low = HD * (h % 2)
                dst = od[:, :, low:low + HD]
                dve.wait_ge(combine_rs, h + 1)
                dve.tensor_tensor(dst, dst, lam[:, 4:8].rearrange("p (t o) -> p t o", o=1).to_broadcast([P, T, HD]),
                                  ALU.mult).then_inc(combined, 1)

            def mixer(mx):
                prob, otok = (prob1, prob2)[mx.b], (otok1, otok2)[mx.b]
                for s in mx.steps:
                    kind, of = s[0], mx.cnt.of[s]
                    if kind in ("proj", "poolproj"):
                        c = mx.c0 + s[1] + 1
                        for q in ([s[2]] if kind == "proj" else [2 * s[2], 2 * s[2] + 1]):
                            split_lo(c, c % 2, q)
                    if kind == "rows" and s not in EARLY:
                        rows_of_projection(mx, s)
                    elif kind == "sum":
                        sum_squares(mx, s)
                    elif kind == "poolproj":
                        dve.wait_ge(products_done, of["product"] + 1)
                        dve.tensor_copy(pool_u[:, s[2], :], ps[:, of["bank"] % 2, :]).then_inc(bank_read, 1)
                    elif kind == "poolmix":
                        dve.wait_ge(products_done, of["product"] + 1)
                        dve.tensor_scalar(mixT[:, s[1], :], ps[:, of["bank"] % 2, :], pool_gain[:, s[1]:s[1] + 1],
                                          None, ALU.mult).then_inc(bank_read, 1)
                    elif kind in ("qkT", "mixT"):
                        read_turned(mx, s, of)
                    elif kind == "out":
                        split_lo(mx.c_out + 1, (mx.c_out + 1) % 2, s[1])
                    elif kind == "out_rows":
                        dve.wait_ge(st_hi_done, mx.st0 + 1)
                        dve.tensor_tensor(out_lo[:, :, :], mixT[:, 0:RB, :], out_hi[:, :, :].bitcast(F32), ALU.subtract)\
                            .then_inc(st_lo_done, 1)
                    elif kind == "decay_abs":
                        decay_abs(mx)
                    elif kind == "decay_ln":
                        dve.wait_ge(decay_exp, 1)
                        dve.tensor_scalar(e_gate, e_gate, 1.0, None, ALU.add).then_inc(decay_sum, 1)
                    elif kind == "decay":
                        decay_rows(of)
                    elif kind == "combine":
                        combine(mx, s[1])
                    elif kind == "combine_scale":
                        combine_scale(s[1])
                    elif kind == "S":
                        (m, t), u = s[1], mx.unit[s[1]]
                        kn = P * (t + 1)
                        dve.wait_ge(scores_done, u + 1)
                        if mx.b == 1 and (m, t) == (0, 0):
                            dve.wait_ge(table_in, 16)
                        if mx.b == 1 and (m, t) == (14, 0):
                            dve.wait_ge(bias_masked, 1)
                        if u >= 3:
                            dve.wait_ge(prob_turned, u - 2)
                        dve.tensor_tensor_reduce(out=prob[:, u % 3, 0:kn], in0=ps[:, 2 + u % 2, 0:kn],
                                                 in1=map_operands(mx.b, m)[3][:, S - kn:S], scale=-1.0, scalar=BIG,
                                                 op0=ALU.add, op1=ALU.min, accum_out=neg_max[:, u % 8:u % 8 + 1])\
                            .then_inc(biased, 1)
                    elif kind == "T":
                        u = mx.unit[s[1]]
                        dve.wait_ge(exp_done, u + 1)
                        link_later(dve.reciprocal(rden[:, u % 8:u % 8 + 1], den[:, u % 8:u % 8 + 1]))
                    elif kind == "PV":
                        (m, t), u = s[1], mx.unit[s[1]]
                        dve.wait_ge(dve_chain, recips[u])
                        dve.wait_ge(pv_done, u + 1)
                        o = ps[:, 6, 0:HD]
                        dve.tensor_scalar(otok[:, m // 2 % 2, t, HD * (m % 2):HD * (m % 2) + HD], o,
                                          rden[:, u % 8:u % 8 + 1], None, ALU.mult).then_inc(o_done, 1)

            recips = []

            def link_later(ins):
                chain[0] += 1
                ins.then_inc(dve_chain, 1)
                recips.append(chain[0])

            def row_products(src, n, c0, g0, st0, start=0):
                def rows_lo(j, slot):
                    dve.wait_ge(st_hi_done, j + (st0 + 1))
                    dve.tensor_tensor(st_lo[:, slot, :, :], src[:, bass.ds(2 * j, RB), :],
                                      st_hi[:, slot, :, :].bitcast(F32), ALU.subtract).then_inc(st_lo_done, 1)

                def chunk(j, jslot, last):
                    for t in range(T):
                        split_lo(c0 + j + 1, (c0 + jslot + 1) % 2, t)
                        if t == 0 and not last:
                            rows_lo(j + 1, (jslot + 1) % 2)

                if start == 0:
                    for t in range(T):
                        split_lo(c0 + 1, (c0 + 1) % 2, t)
                rows_lo(1, 1)
                over_chunks(dve, n, chunk, start=1)

            def first_rows_lo(st0):
                dve.wait_ge(st_hi_done, st0 + 1)
                dve.tensor_tensor(st_lo[:, 0, :, :], hid[:, 0:RB, :], st_hi[:, 0, :, :].bitcast(F32), ALU.subtract)\
                    .then_inc(st_lo_done, 1)

            def swiglu(c0, g0, st0):
                def pair(i, last=False):
                    if last:
                        first_rows_lo(st0)
                    for q in range(4):
                        split_lo(2 * i + (c0 + 1), (c0 + 1) % 2, q)
                    for q in range(4):
                        split_lo(2 * i + (c0 + 2), c0 % 2, q)
                    for m in range(2):
                        dve.wait_ge(gate_silu, 2 * i + (m + 1))
                        dve.wait_ge(products_done, 4 * i + (g0 + m + 3))
                        dve.tensor_tensor(hid[:, bass.ds(2 * i + m, 1), :].rearrange("p o n -> p (o n)"),
                                          act_gate[:, m, :], ps[:, 2 + m, :], ALU.mult).then_inc(hid_done, 1)

                with dve.Fori(0, N_UP // 2 - 1) as i:
                    pair(i)
                pair(N_UP // 2 - 1, last=True)

            def conv_swiglu(c0, g0, st0):
                def taps(dst, m, src, col, ready, count, chain0, done):
                    dve.wait_ge(ready, count)
                    dve.scalar_tensor_tensor(out=dst[:, m, 1:S], in0=src[:, 0:S - 1],
                                             scalar=conv_cols[:, 1, bass.ds(col, 1)], in1=dst[:, m, 1:S],
                                             op0=ALU.mult, op1=ALU.add).then_inc(tap_chain, 1)
                    dve.wait_ge(tap_chain, chain0)
                    return dve.scalar_tensor_tensor(out=dst[:, m, 2:S], in0=src[:, 0:S - 2],
                                                    scalar=conv_cols[:, 0, bass.ds(col, 1)], in1=dst[:, m, 2:S],
                                                    op0=ALU.mult, op1=ALU.add).then_inc(done, 1)

                def pair(i, first=False, last=False):
                    if last:
                        first_rows_lo(st0)
                    for q in range(4):
                        split_lo(2 * i + (c0 + 1), (c0 + 1) % 2, q)
                    if first:
                        dve.wait_ge(small_turned, 2)
                        dve.tensor_copy(conv_cols[:, :, :], ps[:, 6, 0:8 * MT].rearrange("p (j m) -> p j m", j=4))\
                            .then_inc(conv_cols_done, 1)
                        dve.wait_ge(conv_cols_done, 1)
                    for m in range(2):
                        taps(act_gate, m, ps[:, m, :], 2 * i + m, gate_tap, 2 * i + (m + 1), 6 * i + (m + 1), gate_conv)
                    for q in range(4):
                        split_lo(2 * i + (c0 + 2), c0 % 2, q)
                    for m in range(2):
                        taps(act_val, m, ps[:, 2 + m, :], 2 * i + (MT + m), val_tap, 2 * i + (m + 1),
                             6 * i + (2 * m + 3), tap_chain)
                        dve.wait_ge(tap_chain, 6 * i + (2 * m + 4))
                        dve.wait_ge(gate_silu, 2 * i + (MT + m + 1))
                        dve.tensor_tensor(hid[:, bass.ds(2 * i + m, 1), :].rearrange("p o n -> p (o n)"),
                                          act_gate[:, m, :], act_val[:, m, :], ALU.mult).then_inc(hid_done, 1)

                pair(0, first=True)
                with dve.Fori(1, N_UP // 2 - 1) as i:
                    pair(i)
                pair(N_UP // 2 - 1, last=True)

            def during_first_norm(s):
                if s == 2:
                    for q in range(4):
                        split_lo(0, 0, q)
                early_rows(mixers[0], s)

            norm(0, False, 0, during_first_norm)
            mixer(mixers[0])
            link(dve.tensor_tensor(lam_prod[:, :, :], lam_in[:, :, 0, :], lam_in[:, :, 1, :], ALU.mult))
            dve.tensor_reduce(lam[:, 0:2], lam_prod[:, :, :], AX, ALU.add).then_inc(lam_sum, 1)
            dve.tensor_scalar(gcol[:, 0:6:2], gcol[:, 0:6:2], 0.125, None, ALU.mult)
            dve.tensor_scalar(gcol[:, 6:7], gcol[:, 6:7], DIFF_SCALE, None, ALU.mult)
            dve.wait_ge(heads_in, 16 * N_HEADS)
            dve.tensor_scalar(fcol[0:HD, 0:1], fcol[0:HD, 0:1], 0.125, None, ALU.mult)
            dve.wait_ge(lam_exp, 1)
            link(dve.scalar_tensor_tensor(out=lam[:, 2:3], in0=lam[:, 3:4], scalar=-LAM_INIT, in1=lam[:, 2:3],
                                          op0=ALU.add, op1=ALU.subtract))
            dve.wait_ge(bank_read, n1.n["bank"])
            dve.wait_ge(slot_read, n1.n["turn"])
            row_products(mixT, N_OUT, C_OUT1, G_OUT1, 0, start=1)
            norm(1, True, G_UP1 - T)
            swiglu(C_UP1, G_UP1, N_OUT)
            dve.wait_ge(hid_done, MT)
            row_products(hid, N_DOWN, C_DOWN1, G_DOWN1, N_OUT)
            norm(2, True, G_MIX2 - T, lambda s: early_rows(mixers[1], s))
            mixer(mixers[1])
            dve.wait_ge(bank_read, n2.n["bank"])
            dve.wait_ge(slot_read, n2.n["turn"])
            row_products(mixT, N_OUT, C_OUT2, G_OUT2, N_OUT + N_DOWN, start=1)
            norm(3, False, G_UP2 - T)
            conv_swiglu(C_UP2, G_UP2, 2 * N_OUT + N_DOWN)
            dve.wait_ge(hid_done, 2 * MT)
            row_products(hid, N_DOWN, C_DOWN2, G_DOWN2, 2 * N_OUT + N_DOWN)
            n_st = 2 * (N_OUT + N_DOWN)
            dve.wait_ge(st_hi_done, n_st + 1)
            dve.tensor_tensor(st_lo[:, 1, :, :], pT[:, :, :], st_hi[:, 1, :, :].bitcast(F32), ALU.subtract)\
                .then_inc(st_lo_done, 1)

            def gate_weights(s):
                if 1 <= s <= T:
                    split_lo(C_GATE, C_GATE % 2, s - 1)

            norm(4, False, G_PP - T, gate_weights)
            for j in range(D // CW):
                for t in range(T):
                    n = T * j + t
                    if j + 1 < D // CW:
                        split_lo(C_GATE + j + 1, (C_GATE + j + 1) % 2, t)
                    dve.wait_ge(pp_done, t + 1)
                    dve.wait_ge(sig_done, n + 1)
                    link(dve.tensor_tensor(sig[:, n % 2, :], sig[:, n % 2, :], pp[:, t, CW * j:CW * j + CW], ALU.mult))
                    xs = x[:, t, CW * j:CW * j + CW]
                    dve.tensor_tensor(xs, xs, sig[:, n % 2, :], ALU.add).then_inc(final_done, 1)

        @block.tensor
        def _(pe):
            def products(out_, pairs):
                for n, (s_hi, s_lo, m_hi, m_lo) in enumerate(pairs):
                    pe.matmul(out_, s_hi, m_hi, start=(n == 0), stop=False)
                    pe.matmul(out_, s_hi, m_lo, start=False, stop=False)
                    mm = pe.matmul(out_, s_lo, m_hi, start=False, stop=(n == len(pairs) - 1))
                return mm

            def turn(b, t):
                n = T * b + t
                pe.wait_ge(h_tok_done, n + 1)
                for k in range(KB):
                    tr = pe.transpose(turned_rows(t)[:, k, :], h_tok[:, n % 2, P * k:P * k + P], ident[:, :])
                tr.then_inc(h_turned, 1)

            def turn_ahead(b, t):
                for t2 in ((0, 1), (2,), (3,), ())[t]:
                    turn(b, t2)

            def projection(bank, t, slot):
                _, hi, lo = by_cols(slot)
                tok = slice(P * t, P * t + P)
                return products(ps[:, bank, 0:CW],
                                [(h_hi[:, k, tok], h_lo[:, k, tok], hi[:, k, :], lo[:, k, :])
                                 for k in range(KB)])

            def turned_projection(bank, m, slot):
                _, hi, lo = by_cols(slot)
                col = slice(P * m, P * m + P)
                return products(ps[:, bank, :], [(hi[:, k, col], lo[:, k, col], h_hi[:, k, :], h_lo[:, k, :])
                                                 for k in range(KB)])

            def mixer(mx):
                prob, probT, work = (prob1, prob2)[mx.b], (probT1, probT2)[mx.b], (work1, work2)[mx.b]
                for s in mx.steps:
                    kind, of = s[0], mx.cnt.of[s]
                    if kind in ("proj", "poolproj", "poolmix"):
                        if kind == "proj" and s[1] == 0:
                            turn_ahead(mx.norm, s[2])
                        if kind != "poolmix":
                            c = mx.c0 + s[1]
                            if s[2] == 0:
                                pe.wait_ge(lo_done, 4 * (c + 1))
                            pe.wait_ge(h_lo_done, T * mx.norm + (s[2] + 1 if kind == "proj" else T))
                        if of["bank"] >= 2:
                            pe.wait_ge(bank_read, of["bank"] - 1)
                    if kind == "proj":
                        projection(of["bank"] % 2, s[2], c % 2).then_inc(products_done, 1)
                    elif kind == "poolproj":
                        turned_projection(of["bank"] % 2, s[2], c % 2).then_inc(products_done, 1)
                    elif kind == "poolmix":
                        pe.wait_ge(pool_out, s[1] + 1)
                        pe.wait_ge(heads_in, 16 * N_HEADS)
                        pe.matmul(ps[:, of["bank"] % 2, :], pool_w[:, s[1], :], pool_d[:, s[1], :],
                                  start=True, stop=True).then_inc(products_done, 1)
                    elif kind == "out":
                        n = mx.cnt.n
                        for sem_, v in (((bank_read, n["bank"]),), ((biased, n["unit"]),), ((probT_done, n["unit"]),),
                                        ((o_done, n["unit"]), (slot_read, n["turn"])))[s[1]]:
                            pe.wait_ge(sem_, v)
                        pe.wait_ge(lo_done, 4 * (mx.c_out + 1))
                        pe.wait_ge(st_lo_done, mx.st0 + 1)
                        row_tile(s[1], out_hi, out_lo, mx.c_out % 2, True, False).then_inc(products_done, 1)
                    elif kind in ("qkT", "mixT", "decay"):
                        if of["turn"] >= 1:
                            pe.wait_ge(slot_read, of["turn"])
                        if kind == "qkT":
                            r = mx.rows[s[1], s[2]]
                            if r == 0:
                                pe.wait_ge(h_lo_done, T * (mx.norm + 1))
                            pe.wait_ge(bank_read, mx.cnt.of["proj", s[1], s[2]]["bank"] + 1)
                            if mx.chunks[s[1]][0] == "fox_qk":
                                for j in range(4):
                                    col = (HD + 2) * j
                                    tr = pe.transpose(ps[0:HD + 2, 7, P * j:P * j + P],
                                                      work[:, r % 2, col:col + HD + 2], ident[:, :])
                            else:
                                for j in range(2):
                                    tr = pe.transpose(ps[:, 7, P * j:P * j + P], work[:, r % 2, P * j:P * j + P],
                                                      ident[:, :])
                            tr.then_inc(turned, 1)
                        elif kind == "mixT":
                            src, last = row_source(mx.b, s[1])
                            if last is None:
                                pe.wait_ge(combined, 2 * s[1] + 2)
                            else:
                                pe.wait_ge(o_done, mx.unit[last] + 1)
                            for t in range(T):
                                tr = pe.transpose(ps[:, 7, P * t:P * t + P], src[:, t, :], ident[:, :])
                            tr.then_inc(turned, 1)
                        else:
                            pe.wait_ge(constants_set, 2)
                            pe.wait_ge(decay_log, 1)
                            z = decay[:, 0, :, :].rearrange("p t h -> p (t h)")
                            pe.matmul(ps[:, 7, 0:6 * T], tri[:, :], z, start=True, stop=False, skip_group_check=True)
                            for j in range(T - 1):
                                later = ps[:, 7, 6 * (j + 1):6 * T].rearrange("p (t h) -> p t h", h=6)
                                mm = pe.matmul(later, ones[:, :], decay[:, 0, j:j + 1, :].to_broadcast([P, T - 1 - j, 6]),
                                               start=False, stop=(j == T - 2), skip_group_check=True)
                            mm.then_inc(turned, 1)
                    elif kind == "S":
                        (m, t), u = s[1], mx.unit[s[1]]
                        q, k, _, _ = map_operands(mx.b, m)
                        if t == 0:
                            pe.wait_ge(slot_read, rows_turned(mx, m))
                        if u >= 2:
                            pe.wait_ge(biased, u - 1)
                        pe.matmul(ps[:, 2 + u % 2, 0:P * (t + 1)], q[:, P * t:P * t + P], k[:, 0:P * (t + 1)],
                                  start=True, stop=True).then_inc(scores_done, 1)
                    elif kind == "T":
                        (m, t), u = s[1], mx.unit[s[1]]
                        pe.wait_ge(exp_done, u + 1)
                        if u >= 2:
                            pe.wait_ge(probT_done, u - 1)
                        for j in range(t + 1):
                            tr = pe.transpose(ps[:, 4 + u % 2, P * j:P * j + P], prob[:, u % 3, P * j:P * j + P],
                                              ident[:, :])
                        tr.then_inc(prob_turned, 1)
                    elif kind == "PV":
                        (m, t), u = s[1], mx.unit[s[1]]
                        v = map_operands(mx.b, m)[2]
                        if t == 0:
                            pe.wait_ge(bank_read, values_read(mx, m))
                        pe.wait_ge(probT_done, u + 1)
                        if u >= 1:
                            pe.wait_ge(o_done, u)
                        for j in range(t + 1):
                            mm = pe.matmul(ps[:, 6, 0:HD],
                                           probT[:, u % 2, P * j:P * j + P], v[:, j, :], start=(j == 0), stop=(j == t))
                        mm.then_inc(pv_done, 1)

            def row_tile(t, rows_hi, rows_lo, slot, first, last):
                _, hi, lo = by_rows(slot)
                tok = slice(P * t, P * t + P)
                for k in range(RB):
                    for half in range(2):
                        col = slice(512 * half, 512 * half + 512)
                        bank = ps[:, 2 * t + half, :]
                        pe.matmul(bank, rows_hi[:, k, tok], hi[:, k, col], start=first and k == 0, stop=False,
                                  skip_group_check=True)
                        pe.matmul(bank, rows_hi[:, k, tok], lo[:, k, col], start=False, stop=False,
                                  skip_group_check=True)
                        mm = pe.matmul(bank, rows_lo[:, k, tok], hi[:, k, col], start=False,
                                       stop=last and k == RB - 1, skip_group_check=True)
                return mm

            def row_products(n, c0, st0, start=0, order=range(T), bank_waits={}):
                def chunk(j, jslot, last, first=False):
                    pe.wait_ge(lo_done, 4 * j + 4 * (c0 + 1))
                    pe.wait_ge(st_lo_done, j + (st0 + 1))
                    js = jslot % 2
                    for t in (order if first else range(T)):
                        if first:
                            for s, v in bank_waits.get(t, ()):
                                pe.wait_ge(s, v)
                        row_tile(t, st_hi[:, js], st_lo[:, js], (c0 + jslot) % 2, first, last)\
                            .then_inc(products_done, 1)

                if start == 0:
                    chunk(0, 0, n == 1, first=True)
                over_chunks(pe, n, chunk, start=1)

            def up_products(c0, b, gate_read, gate0, hid0, small_turns=None):
                def gates_of_half(m, half):
                    _, hi, lo = by_cols(c0 % 2)
                    tok, col = slice(256 * half, 256 * half + 256), slice(P * m, P * m + P)
                    return products(ps[:, m, tok], [(hi[:, k, col], lo[:, k, col], h_hi[:, k, tok], h_lo[:, k, tok])
                                                    for k in range(KB)])

                def pair(i, first):
                    for which in range(2):
                        pe.wait_ge(lo_done, 8 * i + 4 * (c0 + which + 1))
                        for m in range(2):
                            if not first:
                                if which == 0:
                                    pe.wait_ge(gate_read, 2 * i + (gate0 + m - 1))
                                else:
                                    pe.wait_ge(hid_done, 2 * i + (hid0 + m - 1))
                            if not (first and which == 0):
                                turned_projection(2 * which + m, m, (c0 + which) % 2).then_inc(products_done, 1)
                        if first and which == 0:
                            for t in range(3):
                                turn(b, t)
                            pe.wait_ge(h_lo_done, T * b + 2)
                            gates_of_half(0, 0)
                            turn(b, 3)
                            gates_of_half(1, 0)
                            pe.wait_ge(h_lo_done, T * b + T)
                            if small_turns:
                                small_turns()
                            for m in range(2):
                                gates_of_half(m, 1).then_inc(products_done, 1)

                pair(0, True)
                with pe.Fori(1, N_UP // 2) as i:
                    pair(i, False)

            def turn_small():
                pe.wait_ge(p_in, 16)
                for t in range(T):
                    for k in range(RB):
                        tr = pe.transpose(ps[:, 4 + k, P * t:P * t + P], p_tok[:, t, P * k:P * k + P], ident[:, :])
                tr.then_inc(small_turned, 1)
                pe.wait_ge(conv_in, 32)
                for j in range(4):
                    tr = pe.transpose(ps[:, 6, 2 * MT * j:2 * MT * j + 2 * MT], conv_rows[:, j, :],
                                      ident[0:2 * MT, 0:2 * MT])
                tr.then_inc(small_turned, 1)

            pe.wait_ge(constants_set, 1)
            mixer(mixers[0])
            row_products(N_OUT, C_OUT1, 0, start=1)
            up_products(C_UP1, 1, gate_silu, 0, 0)
            row_products(N_DOWN, C_DOWN1, N_OUT, order=(2, 3, 0, 1),
                         bank_waits={0: [(gate_silu, MT)], 1: [(hid_done, MT)]})
            mixer(mixers[1])
            row_products(N_OUT, C_OUT2, N_OUT + N_DOWN, start=1)
            up_products(C_UP2, 3, gate_conv, 0, MT, turn_small)
            row_products(N_DOWN, C_DOWN2, 2 * N_OUT + N_DOWN, order=(2, 3, 0, 1),
                         bank_waits={2: [(pT_done, 1)], 3: [(conv_cols_done, 1)],
                                     0: [(gate_conv, MT)], 1: [(hid_done, 2 * MT)]})
            pe.wait_ge(lo_done, 4 * (C_PP + 1))
            pe.wait_ge(st_lo_done, 2 * (N_OUT + N_DOWN) + 1)
            for t in range(T):
                turn_ahead(4, t)
                pe.wait_ge(h_lo_done, 4 * T + t + 1)
                row_tile(t, st_hi[:, 1], st_lo[:, 1], C_PP % 2, True, True).then_inc(products_done, 1)
            for j in range(D // CW):
                for t in range(T):
                    n = T * j + t
                    if t == 0:
                        pe.wait_ge(lo_done, 4 * (C_GATE + j + 1))
                    if n < 8:
                        pe.wait_ge(pp_done, n // 2 + 1)
                    else:
                        pe.wait_ge(sig_done, n - 7)
                    projection(n % 8, t, (C_GATE + j) % 2).then_inc(products_done, 1)


_INS = ['x', 'ln_pre_mix', 'w_in', 'w_pool', 'pool_scale', 'w_out', 'ln_post_mix', 'ln_pre_ffn', 'w_gate',
        'w_up', 'w_down', 'ln_post_ffn', 'p_2', 'ln_mix_2', 'w_in_2', 'qk_gain_2', 'lam_params_2', 'subln_gain_2',
        'fgate_bias_2', 'w_out_2', 'ln_ffn_2', 'w_up_2', 'conv_w_2', 'conv_b_2', 'w_down_2', 'ln_ple_2',
        'w_ple_gate_2', 'w_ple_proj_2']


def _constants():
    f32 = np.float32
    q, k = np.arange(P)[:, None], np.arange(S)[None, :] - (S - P)
    dist = q - k
    seen = dist >= 0
    count = (seen & (dist <= 128)).astype(int) + (seen & (dist % 4 == 0)) + (seen & (dist % 16 == 0))
    log_count = np.where(count > 0, np.log(np.maximum(count, 1)), MASKED)
    allowed = (k + S) // HD <= (q + S) // HD
    slopes = [2.0 ** (-8.0 * (h + 1) / 4) for h in range(4)]
    alibi = np.stack([np.where(allowed, -s * np.abs(dist), MASKED) for s in slopes], axis=1)
    freqs = f32(10000.0) ** (-np.arange(HD // 2, dtype=f32) * f32(2.0 / HD))
    ang = (np.arange(S, dtype=f32)[:, None] * freqs[None, :]).reshape(T, P, HD // 2).transpose(1, 0, 2)
    cos, sin = np.cos(ang), np.sin(ang)
    wins = np.array([2, 4, 8, 16]).repeat(HD).reshape(2, P).T[:, :, None]
    return {
        "log_count": log_count.astype(f32),
        "causal": np.where(seen, 0.0, MASKED).astype(f32),
        "alibi": alibi.astype(f32),
        "rope_cos": np.concatenate([cos, cos], axis=-1).astype(f32),
        "rope_sin": np.concatenate([-sin, sin], axis=-1).astype(f32),
        "pool_inv": (f32(1.0) / np.minimum(np.arange(16) + 1, wins)).astype(f32),
    }


def kernel(**inputs):
    import concourse.bacc as _bacc
    from concourse.bass_utils import run_bass_kernel_spmd as _run

    nc = _bacc.Bacc("TRN2", target_bir_lowering=False, num_devices=1)
    given = {name: np.ascontiguousarray(inputs[name]) for name in _INS}
    dist = np.arange(P)[:, None] - (np.arange(S)[None, :] - (S - P))
    rel = np.asarray(inputs["rel_bias_2"])[0]
    given["rel_table"] = np.ascontiguousarray(rel[:, np.clip(dist, -P, P) + P].transpose(1, 0, 2))
    given.update(_constants())
    arrays, A = {}, {}
    for name, a in given.items():
        arrays[f"in_{name}_dram"] = a
        A[name] = nc.dram_tensor(f"in_{name}_dram", a.shape, mybir.dt.from_np(a.dtype), kind="ExternalInput").ap()
    out = nc.dram_tensor("out_0_dram", (1, S, D), F32, kind="ExternalOutput").ap()
    two_blocks_kernel(nc, A, out)
    r = _run(nc, [arrays], core_ids=[0])
    return r.results[0]["out_0_dram"]
```
